# Optimizing a Trainium2 kernel written in Bass

```python
import jax, jax.numpy as jnp
from jax import lax
import numpy as np
import math

D_MODEL = 1024
BATCH = 1
SEQ = 512
DEPTH = 2

N_MIXERS = 2
SB_HEADS = 16
SB_HEAD_DIM = D_MODEL // SB_HEADS
SB_BLOCK = 128
RET_HEADS = 4
RET_QK_DIM = D_MODEL // RET_HEADS
RET_V_DIM = 2 * D_MODEL // RET_HEADS
RET_CHUNK = 128
ROPE_BASE = 10000.0
MLP_HIDDEN = 4 * D_MODEL
RMS_EPS = 1e-6
GN_EPS = 1e-6
N_SB_LAYERS = (DEPTH + N_MIXERS - 1) // N_MIXERS
N_RET_LAYERS = DEPTH // N_MIXERS


F32 = jnp.float32

def rms_norm(x, g):
    xf = x.astype(F32)
    y = xf * lax.rsqrt(jnp.mean(xf * xf, axis=-1, keepdims=True) + RMS_EPS)
    return (y * g.astype(F32)).astype(x.dtype)

def stick_breaking_attention(h, w_in, w_out):
    b, s, _ = h.shape
    q, k, v = jnp.split(h @ w_in, 3, axis=-1)

    def heads(t):
        return t.reshape(b, s, SB_HEADS, SB_HEAD_DIM).transpose(0, 2, 1, 3).astype(F32)

    q, k, v = heads(q), heads(k), heads(v)
    scale = SB_HEAD_DIM ** -0.5
    outs = []
    for blk in range(s // SB_BLOCK):
        start = blk * SB_BLOCK
        end = start + SB_BLOCK
        qb = q[:, :, start:end]
        kp = k[:, :, :end]
        vp = v[:, :, :end]
        z = jnp.einsum('bhqd,bhkd->bhqk', qb, kp) * scale
        t_idx = start + jnp.arange(SB_BLOCK)[:, None]
        s_idx = jnp.arange(end)[None, :]
        mask = s_idx < t_idx
        log_keep = jnp.where(mask, jax.nn.log_sigmoid(-z), 0.0)
        later = lax.cumsum(log_keep, axis=3, reverse=True) - log_keep
        a = jnp.where(mask, jnp.exp(jax.nn.log_sigmoid(z) + later), 0.0)
        outs.append(jnp.einsum('bhqk,bhkd->bhqd', a, vp))
    o = jnp.concatenate(outs, axis=2)
    o = o.transpose(0, 2, 1, 3).reshape(b, s, D_MODEL).astype(h.dtype)
    return o @ w_out

def rotary(x, pos):
    half = x.shape[-1] // 2
    inv_freq = 1.0 / (ROPE_BASE ** jnp.linspace(0.0, 1.0, half, dtype=F32))
    ang = pos.astype(F32)[:, None] * inv_freq[None, :]
    cos, sin = jnp.cos(ang), jnp.sin(ang)
    x1, x2 = x[..., :half], x[..., half:]
    return jnp.concatenate([x1 * cos - x2 * sin, x1 * sin + x2 * cos], axis=-1)

def retention(h, w_in, w_out):
    b, s, _ = h.shape
    c = RET_CHUNK
    nc = s // c
    q, k, v, g = jnp.split(h @ w_in, [D_MODEL, 2 * D_MODEL, 4 * D_MODEL], axis=-1)
    q = q.reshape(b, s, RET_HEADS, RET_QK_DIM).transpose(0, 2, 1, 3).astype(F32)
    k = k.reshape(b, s, RET_HEADS, RET_QK_DIM).transpose(0, 2, 1, 3).astype(F32)
    v = v.reshape(b, s, RET_HEADS, RET_V_DIM).transpose(0, 2, 1, 3).astype(F32)
    pos = jnp.arange(s)
    q = rotary(q, pos)
    k = rotary(k, pos) * (RET_QK_DIM ** -0.5)

    log_gamma = jnp.log1p(-jnp.exp2(-5.0 - jnp.arange(RET_HEADS, dtype=F32)))
    idx = jnp.arange(c, dtype=F32)
    rel = idx[:, None] - idx[None, :]
    decay_in = jnp.where(rel >= 0, jnp.exp(log_gamma[:, None, None] * jnp.maximum(rel, 0.0)), 0.0)
    q_decay = jnp.exp(log_gamma[:, None] * (idx + 1.0))[None, :, :, None]
    k_decay = jnp.exp(log_gamma[:, None] * (c - 1.0 - idx))[None, :, :, None]
    chunk_decay = jnp.exp(log_gamma * c)[None, :, None, None]

    qc = q.reshape(b, RET_HEADS, nc, c, RET_QK_DIM)
    kc = k.reshape(b, RET_HEADS, nc, c, RET_QK_DIM)
    vc = v.reshape(b, RET_HEADS, nc, c, RET_V_DIM)

    scores = jnp.einsum('bhnid,bhnjd->bhnij', qc, kc) * decay_in[None, :, None]
    inner = jnp.einsum('bhnij,bhnje->bhnie', scores, vc)

    def step(state, xs):
        q_n, k_n, v_n = xs
        cross = jnp.einsum('bhid,bhde->bhie', q_n, state) * q_decay
        state = state * chunk_decay + jnp.einsum('bhjd,bhje->bhde', k_n * k_decay, v_n)
        return state, cross

    state0 = jnp.zeros((b, RET_HEADS, RET_QK_DIM, RET_V_DIM), F32)
    xs = (qc.transpose(2, 0, 1, 3, 4), kc.transpose(2, 0, 1, 3, 4), vc.transpose(2, 0, 1, 3, 4))
    _, cross = lax.scan(step, state0, xs)
    o = (inner + cross.transpose(1, 2, 0, 3, 4)).reshape(b, RET_HEADS, s, RET_V_DIM)

    mu = jnp.mean(o, axis=-1, keepdims=True)
    var = jnp.mean(jnp.square(o - mu), axis=-1, keepdims=True)
    o = (o - mu) * lax.rsqrt(var + GN_EPS)
    o = o.transpose(0, 2, 1, 3).reshape(b, s, RET_HEADS * RET_V_DIM)
    y = jax.nn.silu(g.astype(F32)) * o
    return y.astype(h.dtype) @ w_out

def squared_relu_mlp(h, w_up, w_down):
    u = jax.nn.relu(h @ w_up)
    return (u * u) @ w_down

def first_inputs(seed: int = 0) -> dict:
    key = jax.random.key(seed)
    ks = jax.random.split(key, 11)

    def w(k, shape, fan_in):
        return jax.random.normal(k, shape, F32) * (fan_in ** -0.5)

    def gain(k, shape):
        return 1.0 + 0.05 * jax.random.normal(k, shape, F32)

    return {
        "x": jax.random.normal(ks[0], (BATCH, SEQ, D_MODEL), F32),
        "w_sb_in": w(ks[1], (N_SB_LAYERS, D_MODEL, 3 * D_MODEL), D_MODEL),
        "w_sb_out": w(ks[2], (N_SB_LAYERS, D_MODEL, D_MODEL), D_MODEL),
        "w_ret_in": w(ks[3], (N_RET_LAYERS, D_MODEL, 6 * D_MODEL), D_MODEL),
        "w_ret_out": w(ks[4], (N_RET_LAYERS, 2 * D_MODEL, D_MODEL), 2 * D_MODEL),
        "g_mix": gain(ks[5], (DEPTH, D_MODEL)),
        "g_mlp": gain(ks[6], (DEPTH, D_MODEL)),
        "w_mlp_up": w(ks[7], (DEPTH, D_MODEL, MLP_HIDDEN), D_MODEL),
        "w_mlp_down": w(ks[8], (DEPTH, MLP_HIDDEN, D_MODEL), MLP_HIDDEN),
        "g_final": gain(ks[9], (D_MODEL,)),
    }

def first_block(x, w_sb_in, w_sb_out, w_ret_in, w_ret_out, g_mix, g_mlp, w_mlp_up, w_mlp_down, g_final):
    h = x
    for layer in range(DEPTH):
        hn = rms_norm(h, g_mix[layer])
        i = layer // N_MIXERS
        if layer % N_MIXERS == 0:
            h = h + stick_breaking_attention(hn, w_sb_in[i], w_sb_out[i])
        else:
            h = h + retention(hn, w_ret_in[i], w_ret_out[i])
        h = h + squared_relu_mlp(rms_norm(h, g_mlp[layer]), w_mlp_up[layer], w_mlp_down[layer])
    return rms_norm(h, g_final)


DEPTH_2 = 1

CHUNK = 64
EPS = 1e-6
ATT_HEADS = 8
ATT_KV_HEADS = 2
ATT_HEAD_DIM = 64
IDX_HEADS = 8
IDX_HEAD_DIM = 64
TOPK_MAX = 256
Q_BLOCK = 128
MLSTM_HEADS = 4
MLSTM_QK_DIM = 64
MLSTM_V_DIM = 128
CONV_WIDTH = 4
MIX_A = ATT_HEADS * ATT_HEAD_DIM
MIX_B = MLSTM_HEADS * MLSTM_V_DIM
D_FF = 2816
SPLIT_WIDTHS = (
    ATT_HEADS * ATT_HEAD_DIM,
    ATT_KV_HEADS * ATT_HEAD_DIM,
    ATT_KV_HEADS * ATT_HEAD_DIM,
    IDX_HEADS * IDX_HEAD_DIM,
    IDX_HEAD_DIM,
    IDX_HEADS,
    MIX_B,
    MIX_B,
    MLSTM_HEADS,
    MLSTM_HEADS,
    MIX_B,
    D_MODEL,
    D_MODEL,
)
D_IN = sum(SPLIT_WIDTHS)


def rms_norm_2(x, g):
    xf = x.astype(jnp.float32)
    y = xf * lax.rsqrt(jnp.mean(xf * xf, axis=-1, keepdims=True) + EPS)
    return (y * g.astype(jnp.float32)).astype(x.dtype)

def swiglu_ffn(x, g, w_gate, w_up, w_down):
    h = rms_norm_2(x, g)
    return (jax.nn.silu(h @ w_gate) * (h @ w_up)) @ w_down

def split_columns(p):
    parts, off = [], 0
    for w in SPLIT_WIDTHS:
        parts.append(p[..., off:off + w])
        off += w
    return parts

def dsa_attention(q, k, v, iq, ik, iw):
    B, S = q.shape[0], q.shape[1]
    k_sel = min(TOPK_MAX, S // 4)
    nb = S // Q_BLOCK
    reps = ATT_HEADS // ATT_KV_HEADS
    idx_scale = (IDX_HEAD_DIM ** -0.5) * (IDX_HEADS ** -0.5)
    att_scale = ATT_HEAD_DIM ** -0.5
    key_pos = jnp.arange(S)

    qb = q.reshape(B, nb, Q_BLOCK, ATT_KV_HEADS, reps, ATT_HEAD_DIM).transpose(1, 0, 2, 3, 4, 5)
    iqb = iq.reshape(B, nb, Q_BLOCK, IDX_HEADS, IDX_HEAD_DIM).transpose(1, 0, 2, 3, 4)
    iwb = iw.reshape(B, nb, Q_BLOCK, IDX_HEADS).transpose(1, 0, 2, 3)
    ids = jnp.arange(nb, dtype=jnp.int32)

    def block(args):
        q_blk, iq_blk, iw_blk, bi = args
        t = bi * Q_BLOCK + jnp.arange(Q_BLOCK)
        logits = jnp.einsum('bqhd,bsd->bqhs', iq_blk, ik)
        score = jnp.einsum('bqhs,bqh->bqs', jax.nn.relu(logits), iw_blk).astype(jnp.float32) * idx_scale
        limit = (t // CHUNK + 1) * CHUNK
        allowed = key_pos[None, :] < limit[:, None]
        score = jnp.where(allowed[None], score, -jnp.inf)
        top_s, top_i = lax.top_k(score, k_sel)
        valid = jnp.isfinite(top_s)
        kg = jax.vmap(lambda kb, ib: kb[ib])(k, top_i)
        vg = jax.vmap(lambda vb, ib: vb[ib])(v, top_i)
        s = jnp.einsum('bqgrd,bqkgd->bqgrk', q_blk, kg).astype(jnp.float32) * att_scale
        s = jnp.where(valid[:, :, None, None, :], s, -jnp.inf)
        p = jax.nn.softmax(s, axis=-1).astype(vg.dtype)
        return jnp.einsum('bqgrk,bqkgd->bqgrd', p, vg)

    o = lax.map(block, (qb, iqb, iwb, ids))
    return o.transpose(1, 0, 2, 3, 4, 5).reshape(B, S, MIX_A)

def mlstm_branch(xm, vm, ig, fg, o_pre, conv_w, conv_b, w_mq, w_mk, b_i, b_f, head_g):
    B, S, _ = xm.shape
    H, L = MLSTM_HEADS, CHUNK
    nc = S // L
    xpad = jnp.pad(xm, ((0, 0), (CONV_WIDTH - 1, 0), (0, 0)))
    xc = conv_b + xpad[:, 0:S] * conv_w[0]
    for j in range(1, CONV_WIDTH):
        xc = xc + xpad[:, j:j + S] * conv_w[j]
    xc = jax.nn.silu(xc).reshape(B, S, H, MLSTM_V_DIM)
    q = jnp.einsum('bshc,hcd->bshd', xc, w_mq).astype(jnp.float32) * (MLSTM_QK_DIM ** -0.5)
    k = jnp.einsum('bshc,hcd->bshd', xc, w_mk).astype(jnp.float32)
    v = vm.reshape(B, S, H, MLSTM_V_DIM).astype(jnp.float32)
    log_i = (ig + b_i).astype(jnp.float32)
    log_f = jax.nn.log_sigmoid((fg + b_f).astype(jnp.float32))

    def to_chunks(a):
        a = a.reshape((B, nc, L) + a.shape[2:])
        perm = (1, 0, 3, 2) + tuple(range(4, a.ndim))
        return a.transpose(perm)

    tril = jnp.tril(jnp.ones((L, L), dtype=bool))

    def step(carry, inp):
        C, n, m = carry
        qc, kc, vc, ic, fc = inp
        b = jnp.cumsum(fc, axis=-1)
        D = b[..., :, None] - b[..., None, :] + ic[..., None, :]
        D = jnp.where(tril, D, -jnp.inf)
        inter = b + m[..., None]
        m_t = jnp.maximum(jnp.max(D, axis=-1), inter)
        W = jnp.einsum('bhtd,bhsd->bhts', qc, kc) * jnp.exp(D - m_t[..., None])
        w_int = jnp.exp(inter - m_t)
        num = jnp.einsum('bhts,bhsv->bhtv', W, vc) + w_int[..., None] * jnp.einsum('bhtd,bhdv->bhtv', qc, C)
        den = jnp.sum(W, axis=-1) + w_int * jnp.einsum('bhtd,bhd->bht', qc, n)
        h = num / jnp.maximum(jnp.abs(den), jnp.exp(-m_t))[..., None]
        bL = b[..., -1]
        wk = bL[..., None] - b + ic
        m_new = jnp.maximum(bL + m, jnp.max(wk, axis=-1))
        ws = jnp.exp(wk - m_new[..., None])
        wc = jnp.exp(bL + m - m_new)
        C_new = wc[..., None, None] * C + jnp.einsum('bhs,bhsd,bhsv->bhdv', ws, kc, vc)
        n_new = wc[..., None] * n + jnp.einsum('bhs,bhsd->bhd', ws, kc)
        return (C_new, n_new, m_new), h

    init = (jnp.zeros((B, H, MLSTM_QK_DIM, MLSTM_V_DIM), jnp.float32),
            jnp.zeros((B, H, MLSTM_QK_DIM), jnp.float32),
            jnp.zeros((B, H), jnp.float32))
    _, hs = lax.scan(step, init, (to_chunks(q), to_chunks(k), to_chunks(v), to_chunks(log_i), to_chunks(log_f)))
    h = hs.transpose(1, 0, 3, 2, 4).reshape(B, S, H, MLSTM_V_DIM)
    h = rms_norm_2(h, head_g.reshape(H, MLSTM_V_DIM)).reshape(B, S, MIX_B).astype(xm.dtype)
    return h * jax.nn.sigmoid(o_pre)

def second_inputs(seed: int = 0) -> dict:
    key = jax.random.key(seed)
    ks = jax.random.split(key, 32)
    f32 = jnp.float32

    def nrm(k, shape, fan_in):
        return jax.random.normal(k, shape, f32) * (fan_in ** -0.5)

    def gain(k, shape):
        return 1.0 + 0.02 * jax.random.normal(k, shape, f32)

    Ld = DEPTH_2
    return {
        "x": jax.random.normal(ks[0], (BATCH, SEQ, D_MODEL), f32),
        "ffn1_norm": gain(ks[1], (Ld, D_MODEL)),
        "ffn1_w_gate": nrm(ks[2], (Ld, D_MODEL, D_FF), D_MODEL),
        "ffn1_w_up": nrm(ks[3], (Ld, D_MODEL, D_FF), D_MODEL),
        "ffn1_w_down": nrm(ks[4], (Ld, D_FF, D_MODEL), D_FF),
        "mix_norm": gain(ks[5], (Ld, D_MODEL)),
        "w_in": nrm(ks[6], (Ld, D_MODEL, D_IN), D_MODEL),
        "q_norm": gain(ks[7], (Ld, ATT_HEAD_DIM)),
        "k_norm": gain(ks[8], (Ld, ATT_HEAD_DIM)),
        "idx_k_norm": gain(ks[9], (Ld, IDX_HEAD_DIM)),
        "conv_w": nrm(ks[10], (Ld, CONV_WIDTH, MIX_B), CONV_WIDTH),
        "conv_b": 0.02 * jax.random.normal(ks[11], (Ld, MIX_B), f32),
        "w_mq": nrm(ks[12], (Ld, MLSTM_HEADS, MLSTM_V_DIM, MLSTM_QK_DIM), MLSTM_V_DIM),
        "w_mk": nrm(ks[13], (Ld, MLSTM_HEADS, MLSTM_V_DIM, MLSTM_QK_DIM), MLSTM_V_DIM),
        "b_i": 0.1 * jax.random.normal(ks[14], (Ld, MLSTM_HEADS), f32),
        "b_f": 3.0 + 0.1 * jax.random.normal(ks[15], (Ld, MLSTM_HEADS), f32),
        "m_head_norm": gain(ks[16], (Ld, MIX_B)),
        "w_proj_a": nrm(ks[17], (Ld, MIX_A, D_MODEL), MIX_A),
        "w_proj_b": nrm(ks[18], (Ld, MIX_B, D_MODEL), MIX_B),
        "w_out": nrm(ks[19], (Ld, D_MODEL, D_MODEL), D_MODEL),
        "ffn2_norm": gain(ks[20], (Ld, D_MODEL)),
        "ffn2_w_gate": nrm(ks[21], (Ld, D_MODEL, D_FF), D_MODEL),
        "ffn2_w_up": nrm(ks[22], (Ld, D_MODEL, D_FF), D_MODEL),
        "ffn2_w_down": nrm(ks[23], (Ld, D_FF, D_MODEL), D_FF),
    }

def second_block(x, ffn1_norm, ffn1_w_gate, ffn1_w_up, ffn1_w_down, mix_norm, w_in,
              q_norm, k_norm, idx_k_norm, conv_w, conv_b, w_mq, w_mk, b_i, b_f,
              m_head_norm, w_proj_a, w_proj_b, w_out, ffn2_norm, ffn2_w_gate,
              ffn2_w_up, ffn2_w_down):
    B, S, _ = x.shape
    for l in range(DEPTH_2):
        x = x + 0.5 * swiglu_ffn(x, ffn1_norm[l], ffn1_w_gate[l], ffn1_w_up[l], ffn1_w_down[l])
        h = rms_norm_2(x, mix_norm[l])
        (aq, ak, av, iq, ik, iw, mx, mv, mi, mf, mo, ga, gb) = split_columns(h @ w_in[l])
        q = rms_norm_2(aq.reshape(B, S, ATT_HEADS, ATT_HEAD_DIM), q_norm[l])
        k = rms_norm_2(ak.reshape(B, S, ATT_KV_HEADS, ATT_HEAD_DIM), k_norm[l])
        v = av.reshape(B, S, ATT_KV_HEADS, ATT_HEAD_DIM)
        iq = iq.reshape(B, S, IDX_HEADS, IDX_HEAD_DIM)
        ik = rms_norm_2(ik, idx_k_norm[l])
        ya = dsa_attention(q, k, v, iq, ik, iw)
        yb = mlstm_branch(mx, mv, mi, mf, mo, conv_w[l], conv_b[l], w_mq[l], w_mk[l],
                          b_i[l], b_f[l], m_head_norm[l])
        merged = jax.nn.sigmoid(ga) * (ya @ w_proj_a[l]) + jax.nn.sigmoid(gb) * (yb @ w_proj_b[l])
        x = x + merged @ w_out[l]
        x = x + 0.5 * swiglu_ffn(x, ffn2_norm[l], ffn2_w_gate[l], ffn2_w_up[l], ffn2_w_down[l])
    return x


def setup_inputs(seed=0):
    out = dict(first_inputs(seed))
    for name, value in second_inputs(seed + 1).items():
        if name != "x":
            out[name + "_2"] = value
    return out


def reference(
    x, w_sb_in, w_sb_out, w_ret_in, w_ret_out, g_mix, g_mlp, w_mlp_up, w_mlp_down, g_final,
    ffn1_norm_2, ffn1_w_gate_2, ffn1_w_up_2, ffn1_w_down_2, mix_norm_2, w_in_2, q_norm_2,
    k_norm_2, idx_k_norm_2, conv_w_2, conv_b_2, w_mq_2, w_mk_2, b_i_2, b_f_2, m_head_norm_2,
    w_proj_a_2, w_proj_b_2, w_out_2, ffn2_norm_2, ffn2_w_gate_2, ffn2_w_up_2, ffn2_w_down_2,
):
    x = first_block(
        x, w_sb_in, w_sb_out, w_ret_in, w_ret_out, g_mix, g_mlp, w_mlp_up, w_mlp_down, g_final,
    )
    return second_block(
        x, ffn1_norm_2, ffn1_w_gate_2, ffn1_w_up_2, ffn1_w_down_2, mix_norm_2, w_in_2, q_norm_2,
        k_norm_2, idx_k_norm_2, conv_w_2, conv_b_2, w_mq_2, w_mk_2, b_i_2, b_f_2, m_head_norm_2,
        w_proj_a_2, w_proj_b_2, w_out_2, ffn2_norm_2, ffn2_w_gate_2, ffn2_w_up_2, ffn2_w_down_2,
    )


_drawn_inputs = setup_inputs


def setup_inputs(seed=0):
    import zlib

    import numpy as np

    out = dict(_drawn_inputs(seed))
    spreads = {}
    factors = {'ffn1_norm_2': 5.055,
     'mix_norm_2': 3.714,
     'q_norm_2': 27.159,
     'k_norm_2': 27.619,
     'idx_k_norm_2': 26.335,
     'conv_b_2': 5.229,
     'b_i_2': 200.0,
     'b_f_2': 39.256,
     'm_head_norm_2': 47.407,
     'ffn2_norm_2': 21.759}
    for name, (base, spread) in spreads.items():
        noise = np.random.default_rng([zlib.crc32(name.encode()), seed]).standard_normal(out[name].shape)
        drawn = base * np.exp(spread * noise) if base else spread * noise
        out[name] = __import__('jax').numpy.asarray(drawn.astype(out[name].dtype))
    for name, factor in factors.items():
        out[name] = (out[name] * factor).astype(out[name].dtype)
    return out
```

```python
from contextlib import ExitStack

import numpy as np

import concourse.bass as bass
from concourse import mybir

F32 = mybir.dt.float32
F32R = mybir.dt.float32r
ALU = mybir.AluOpType
ACT = mybir.ActivationFunctionType
AX_X = mybir.AxisListType.X

P = 128
T = 512
TB = T // P
D = 1024
DC = D // P
KC = 8
EPS = 1e-6
BIG = 1e30
OUT_OF_REACH = -1e38
TAKEN = -3e38
HIDDEN = 4096
MLP_GROUPS = (KC,) * (HIDDEN // (KC * P))
SB_HEADS, SB_DIM = 16, 64
RET_HEADS, RET_QK, RET_V = 4, 256, 512
D_FF = 2816
FFN_GROUPS = (8, 8, 6)
ATT_HEADS, ATT_KV, ATT_DIM = 8, 2, 64
IDX_HEADS, IDX_DIM = 8, 64
TOPK, CHUNK = 128, 64
ML_HEADS, ML_QK, ML_V, CONV = 4, 64, 128, 4
assert sum(FFN_GROUPS) * P == D_FF and TOPK == min(256, T // 4) and TOPK % 8 == 0

PARAMS, n_param = {}, 0
for _name, _count in (("g_mix0", DC), ("g_mlp0", DC), ("g_mix1", DC), ("g_mlp1", DC), ("g_final", DC),
                      ("ffn1_norm", DC), ("mix_norm", DC), ("ffn2_norm", DC), ("q_norm", 1), ("k_norm", 1),
                      ("idx_k_norm", 1), ("conv_w", 4 * CONV), ("conv_b", 4), ("b_i", 1), ("b_f", 1),
                      ("head_norm", ML_HEADS), ("w_mqk", ML_HEADS * 2 * ML_QK)):
    PARAMS[_name] = (n_param, _count)
    n_param += _count

MIX_K, MIX_Q, MIX_V, MIX_IK, MIX_IQ, MIX_GATES, MIX_MX, MIX_MV, MIX_MO, MIX_BLOCKS = 0, 2, 6, 7, 8, 12, 13, 17, 21, 25
GATE_IW, GATE_I, GATE_F = 0, 32, 64

RET_QKV, RET_G = 8, 4
RUN_AT, N_BLOCKS = {}, 0
for _name, _count in (("sb", 3 * DC), ("sb_out", DC), ("mlp0", 2 * DC * len(MLP_GROUPS)),
                      ("ret", RET_HEADS * (RET_QKV + RET_G)), ("ret_out", 2 * DC),
                      ("mlp1", 2 * DC * len(MLP_GROUPS)), ("ffn1", 2 * D_FF // P + DC * len(FFN_GROUPS)),
                      ("mix", MIX_BLOCKS), ("proj", 3 * DC), ("w_out", DC),
                      ("ffn2", 2 * D_FF // P + DC * len(FFN_GROUPS))):
    RUN_AT[_name] = N_BLOCKS
    N_BLOCKS += _count

HEAD_NORMED = {MIX_K: "k_norm", MIX_K + 1: "k_norm", MIX_IK: "idx_k_norm"} | {MIX_Q + c: "q_norm" for c in range(4)}

NEG_AT = [0, P, 3 * P, 6 * P]

NORMS = [("g_mix0", None), ("g_mlp0", RUN_AT["sb_out"]), ("g_mix1", RUN_AT["ret"] - DC),
         ("g_mlp1", RUN_AT["mlp1"] - DC), ("g_final", RUN_AT["ffn1"] - DC), ("ffn1_norm", None),
         ("mix_norm", RUN_AT["mix"] - DC), ("ffn2_norm", RUN_AT["w_out"])]
N_MIX0, N_MLP0, N_MIX1, N_MLP1, N_FINAL, N_FFN1, N_MIX, N_FFN2 = range(8)

Z_AT = {(0, 0): 0, (0, 1): 512, (0, 3): 896, (0, 2): 1024, (1, 2): 1280, (1, 0): 1536, (1, 1): 2048, (1, 3): 2432}
Z_BANKS = 5
S_AT = {0: 0, 1: 512, 3: 896, 2: 1024}


def seen_by(kb):
    return T - kb * P


def place_of(n):
    return n if isinstance(n, tuple) else (n, None)


def number(n, plus=0):
    c, r = place_of(n)
    return c + plus if r is None else r * 2 + (c + plus)


def later(n, k):
    c, r = place_of(n)
    return (c + k, r)


def slot(n):
    return place_of(n)[0] % 2


def turn(n, plus=0):
    c, r = place_of(n)
    return c // 2 + plus if r is None else r + (c // 2 + plus)


def pairs(eng, first, blocks, body, step=2):
    turns = blocks // step
    assert turns * step == blocks and step % 2 == 0
    if turns == 1:
        body((first, None), None)
        return
    with eng.Fori(0, turns) as t:
        body((first, t * (step // 2)), t)


def at(t, scale, plus):
    return bass.ds(plus if t is None else t * scale + plus, 1)


def flat(ap):
    return ap.rearrange("p a b -> p (a b)")


def build(nc, stream, params, tables, tables_ret, tables_mix, x_in, out):
    with ExitStack() as ctx:
        where = [(nc.sbuf_base + 63) // 64 * 64]

        def sb(name, shape, dt=F32, over=None):
            size = int(np.prod(shape[1:])) * 4
            spot = where[0] if over is None else over
            t = nc.alloc_sbuf_tensor_at(name, shape, dt, offset=spot)
            if over is None:
                where[0] += (size + 31) // 32 * 32
            return t

        def sem(name):
            return ctx.enter_context(nc.semaphore(name))

        h = sb("h", [P, DC, T])
        x_hi = sb("x_hi", [P, DC, T], F32R)
        x_lo_at = where[0]
        x_lo = sb("x_lo", [P, DC, T], F32R)
        squares = sb("squares", [P, DC, T], over=x_lo_at)
        raw = sb("raw", [P, 2, KC, P])
        w_hi = sb("w_hi", [P, 2, KC, P], F32R)
        w_lo = sb("w_lo", [P, 2, KC, P], F32R)
        prm = sb("prm", [P, n_param])
        tab = sb("tab", [P, 4, P])
        ident, neg_tri, strict, head_mean = (tab[:, i] for i in range(4))
        ones = sb("ones", [P, 4, P])
        mean_d, mean_v, one, neg_one = (ones[:, i] for i in range(4))
        eps = sb("eps", [P, 1])
        std = sb("std", [P, T])
        rstd = sb("rstd", [P, T])
        u_sum = rstd
        xn = sb("xn", [P, 2, T])
        arena = where[0]

        def col(name, i=0, rows=P):
            c = PARAMS[name][0] + i
            return prm[0:rows, c:c + 1]

        where[0] = arena
        u_hi = sb("u_hi", [P, 2, KC, T], F32R)
        u_lo = sb("u_lo", [P, 2, KC, T], F32R)
        u_act = sb("u_act", [P, T])
        u = sb("u", [P, 2, T])
        where[0] = arena
        x_tok = sb("x_tok", [P, TB, D])
        where[0] = arena
        o_hi = sb("o_hi", [P, DC, T], F32R)
        o_lo = sb("o_lo", [P, DC, T], F32R)
        sb_q = sb("sb_q", [P, T])
        sb_k = sb("sb_k", [P, T])
        sb_v = sb("sb_v", [P, T])
        sb_vt = sb("sb_vt", [P, TB, P])
        z_sp = sb("z_sp", [P, Z_BANKS, T])
        z_ex = sb("z_ex", [P, Z_BANKS, T])
        where[0] = arena
        y_hi = sb("y_hi", [P, 2 * DC, T], F32R)
        y_lo = sb("y_lo", [P, 2 * DC, T], F32R)
        tab_ret = sb("tab_ret", [P, 2 + RET_HEADS, T])
        r_q = sb("r_q", [P, 2, T])
        r_k = sb("r_k", [P, 2, T])
        r_x = sb("r_x", [P, 2, T])
        r_t = sb("r_t", [P, 2, T])
        r_v = sb("r_v", [P, TB, RET_V])
        r_g = sb("r_g", [P, 4, T])
        r_p = sb("r_p", [P, 1280])
        r_o = sb("r_o", [P, 4, T])
        r_sq = [xn[:, 0], xn[:, 1], r_x[:, 0], r_x[:, 1]]
        ret_end = where[0]
        where[0] = arena
        pj_at = where[0]
        pj = sb("pj", [P, MIX_BLOCKS, T])
        ya_hi = sb("ya_hi", [P, 4, T], F32R)
        ya_lo = sb("ya_lo", [P, 4, T], F32R)
        yb_hi = sb("yb_hi", [P, 4, T], F32R)
        yb_lo = sb("yb_lo", [P, 4, T], F32R)
        tab_mix = sb("tab_mix", [P, 6, P])
        later_keys, mean_h = tab_mix[:, 4], tab_mix[:, 5]
        a_v = sb("a_v", [P, TB, P])
        m_v = sb("m_v", [P, TB, 4 * P])
        iw = sb("iw", [P, TB, IDX_HEADS])
        scratch = where[0]
        n_sq = sb("n_sq", [P, 2, T])
        n_std = sb("n_std", [P, 2, T])
        n_r = sb("n_r", [P, 2, T])
        m_xc = sb("m_xc", [P, 4, T], over=pj_at + MIX_MV * T * 4)
        where[0] = pj_at + MIX_MX * T * 4
        m_q = sb("m_q", [ML_QK, T])
        m_k = sb("m_k", [ML_QK, T])
        m_h = sb("m_h", [P, T])
        m_so = sb("m_so", [P, T])
        where[0] = scratch
        g_li = sb("g_li", [ML_HEADS, T])
        g_lf = sb("g_lf", [ML_HEADS, T])
        g_sum = sb("g_sum", [ML_HEADS, T])
        g_a = sb("g_a", [ML_HEADS, T])
        g_max = sb("g_max", [ML_HEADS, T])
        m_a = sb("m_a", [P, TB, ML_HEADS])
        m_w = sb("m_w", [P, 1280])
        where[0] = scratch
        score = sb("score", [P, T])
        neg = sb("neg", [P, 1280])
        rr = sb("rr", [P, 2, T])
        s_m = sb("s_m", [P, 2, T])
        stat = sb("stat", [P, 4, ATT_HEADS * TB])
        best = sb("best", [P, 8])
        mix_end = where[0]
        where[0] = arena
        mg_hi = sb("mg_hi", [P, DC, T], F32R)
        mg_lo = sb("mg_lo", [P, DC, T], F32R)

        ps = ctx.enter_context(nc.psum_tensor("ps", [P, 8, T], F32))
        GEMM_BANK = 6

        raw_full = [sem("raw_full_0"), sem("raw_full_1")]
        hi_done = sem("hi_done")
        lo_done = sem("lo_done")
        mm_done = sem("mm_done")
        bank_free = [sem("bank_free_0"), sem("bank_free_1")]
        made = {}

        def sig(name):
            if name not in made:
                made[name] = sem(name)
            return made[name]

        block = ctx.enter_context(nc.Block())

        @block.sync
        def _(sp):
            sp.dma_start(x_tok[:], x_in.rearrange("(b p) d -> p b d", p=P)).then_inc(sig("x_in"), 16)
            sp.dma_start(tab[:], tables).then_inc(sig("tables_in"), 16)
            sp.dma_start(prm[:], params).then_inc(sig("tables_in"), 16)

            def load(n):
                sp.wait_ge(lo_done, number(n, 1))
                sp.dma_start(raw[:, slot(n)], stream[bass.ds(number(n), 1)].rearrange(
                    "a p (k m) -> p (a k) m", m=P)).then_inc(raw_full[slot(n)], 16)

            def load_two(n, _):
                load(n)
                load(later(n, 1))

            def load_run(first, last):
                if first % 2:
                    load(first)
                    first += 1
                pairs(sp, first, (last - first) // 2 * 2, load_two)
                if (last - first) % 2:
                    load(last - 1)

            load_run(0, RUN_AT["ret"] - DC)
            sp.wait_ge(sig("ul_done"), HIDDEN // P)
            sp.dma_start(tab_ret[:], tables_ret).then_inc(sig("tables_ret_in"), 16)
            load_run(RUN_AT["ret"] - DC, RUN_AT["mlp1"] + DC)
            sp.wait_ge(mm_done, RUN_AT["mlp1"] + 2 + 1)
            sp.dma_start(tab_mix[:], tables_mix).then_inc(sig("tables_mix_in"), 16)
            load_run(RUN_AT["mlp1"] + DC, N_BLOCKS)
            sp.wait_ge(sig("out_ready"), 2 * TB)
            sp.dma_start(out.rearrange("(b p) d -> p b d", p=P), x_tok[:]).then_inc(sig("stored"), 16)
            sp.wait_ge(sig("stored"), 16)

        @block.scalar
        def _(act):
            def split_hi(n):
                if place_of(n)[1] is None and number(n) >= N_BLOCKS:
                    return
                act.wait_ge(raw_full[slot(n)], turn(n, 1) * 16)
                act.wait_ge(mm_done, number(n, 1))
                nc.scalar.activation(w_hi[:, slot(n)], raw[:, slot(n)], ACT.Copy).then_inc(hi_done, 1)

            def product(n):
                act.wait_ge(mm_done, number(n, 3))
                return ps[:, GEMM_BANK + slot(n)]

            def freed(n):
                act.wait_ge(bank_free[slot(n)], turn(n, 2))

            def move(n, dst, scale=1.0):
                nc.scalar.activation(dst, product(n), ACT.Copy, scale=scale).then_inc(bank_free[slot(n)], 1)

            def norm(k):
                name, first = NORMS[k]
                for c in range(DC):
                    if first is not None:
                        freed(first + c)
                    elif k == N_MIX0:
                        act.wait_ge(sig("h_in"), c + 1)
                    else:
                        act.wait_ge(sig("final_done"), c + 1)
                    nc.scalar.activation(squares[:, c], h[:, c], ACT.Square).then_inc(sig("sq_done"), 1)
                act.wait_ge(sig("ms_done"), k + 1)
                nc.scalar.activation(std[:], ps[:, 5], ACT.Sqrt, bias=eps[:]).then_inc(sig("std_done"), 1)
                if k == N_FINAL:
                    return
                nx = split_norms.index(k)
                for c in range(DC):
                    act.wait_ge(sig("xn_done"), nx * DC + c + 1)
                    nc.scalar.activation(x_hi[:, c], xn[:, c % 2], ACT.Copy).then_inc(sig("xh_done"), 1)

            split_norms = [k for k in range(len(NORMS)) if k != N_FINAL]
            act.wait_ge(sig("consts"), 5)
            split_hi(0)
            norm(N_MIX0)

            def sb_moves(n, which):
                if which == 0:
                    move(n, sb_q[:], SB_DIM ** -0.5)
                else:
                    move(n, sb_k[:] if which == 1 else sb_v[:])

            for which in range(3):
                split_hi(which + 1)
                sb_moves(which, which)

            def sb_pair(n, t, pc, step, dense=True):
                p = pc if t is None else t * step + pc
                if dense:
                    split_hi(later(n, 1))
                for z in range(Z_BANKS):
                    act.wait_ge(sig("abs_done"), p * Z_BANKS + (z + 1))
                    nc.scalar.activation(z_ex[:, z], z_ex[:, z], ACT.Exp, scale=-1.0).then_inc(sig("exp_done"), 1)
                if dense:
                    sb_moves(n, 0)
                    split_hi(later(n, 2))
                for z in range(Z_BANKS):
                    act.wait_ge(sig("exp_done"), p * Z_BANKS + (z + 1))
                    nc.scalar.activation(z_ex[:, z], z_ex[:, z], ACT.Ln, bias=1.0).then_inc(sig("ln_done"), 1)
                if dense:
                    sb_moves(later(n, 1), 1)
                act.wait_ge(sig("cum_done"), p + 1)
                for z in range(Z_BANKS):
                    act.wait_ge(sig("sp_done"), p * Z_BANKS + (z + 1))
                    nc.scalar.activation(z_ex[:, z], ps[:, z], ACT.Exp).then_inc(sig("a_done"), 1)
                if dense:
                    split_hi(later(n, 3))
                    sb_moves(later(n, 2), 2)
                act.wait_ge(sig("av_done"), p + 1)
                nc.scalar.activation(flat(o_hi[:, at(t, step, pc)]), ps[:, 5], ACT.Copy).then_inc(sig("oh_done"), 1)

            def sb_two(n, t):
                sb_pair(n, t, 0, 2)
                sb_pair(later(n, 3), t, 1, 2)

            pairs(act, 3, 6 * 3, sb_two, step=6)
            sb_pair(3 * 7, None, 6, 0)
            sb_pair(None, None, 7, 0, dense=False)

            def ahead(first, blocks):
                def two(n, _):
                    split_hi(later(n, 1))
                    split_hi(later(n, 2))
                if first + blocks == N_BLOCKS:
                    pairs(act, first, blocks - 2, two)
                    two(N_BLOCKS - 2, None)
                else:
                    pairs(act, first, blocks, two)

            ahead(RUN_AT["sb_out"], DC)
            norm(N_MLP0)

            def hidden_hi(t, scale, plus, done, group):
                act.wait_ge(sig("u_done"), done)
                nc.scalar.activation(flat(u_hi[:, group % 2, at(t, scale, plus)]), u[:, plus],
                                     ACT.Copy).then_inc(sig("uh_done"), 1)

            def mlp(first, chunks_before):
                def up(n, t, group, before):
                    for i in range(2):
                        split_hi(later(n, i + 1))
                        nc.scalar.activation(u_act[:], product(later(n, i)), ACT.Relu).then_inc(
                            bank_free[slot(later(n, i))], 1)
                        done = before + i + 1 if t is None else t * 2 + (before + i + 1)
                        hidden_hi(t, 2, i, done, group)
                groups(MLP_GROUPS, first, chunks_before, 1, up)

            def ffn(first, chunks_before):
                def up(n, t, group, before):
                    split_hi(later(n, 1))
                    nc.scalar.activation(u_act[:], product(n), ACT.Silu).then_inc(bank_free[slot(n)], 1)
                    split_hi(later(n, 2))
                    hidden_hi(t, 1, 0, before + 1 if t is None else t + (before + 1), group)
                groups(FFN_GROUPS, first, chunks_before, 2, up)

            def groups(sizes, first, chunks_before, per_chunk, up):
                n = first
                for g in range(len(sizes) + 1):
                    if g < len(sizes):
                        before = chunks_before + sum(sizes[:g])
                        pairs(act, n, sizes[g] * per_chunk, lambda m, t: up(m, t, g, before))
                        n += sizes[g] * per_chunk
                    if g >= 1:
                        ahead(n, DC)
                        n += DC

            mlp(RUN_AT["mlp0"], 0)
            norm(N_MIX1)

            def r_half(n, i, rotated, scale):
                split_hi(later(n, 1))
                if rotated is not None:
                    act.wait_ge(sig("rot_done"), rotated)
                move(n, r_x[:, i], scale)

            def r_value(n, j, transposed):
                split_hi(later(n, 1))
                if transposed is not None:
                    act.wait_ge(sig("rvt_done"), transposed)
                move(n, r_t[:, j % 2])

            def count(t, scale, plus):
                return plus if t is None else t * scale + plus

            def r_qkv(n, t, i):
                for j in range(4):
                    r_half(later(n, j), j % 2, None if t is None and i == 0 and j < 2 else
                           count(t, 2, 2 * i + j // 2), 1.0 if j < 2 else RET_QK ** -0.5)
                act.wait_ge(sig("rot_done"), count(t, 2, 2 * i + 2))
                for j in range(4):
                    r_value(later(n, 4 + j), j, count(t, 4, 4 * i + j - 1) if j >= 2 else None)

            def r_head(n, t, i, dense=True):
                if dense:
                    for j in range(4):
                        r_half(later(n, j), j % 2, count(t, 2, 2 * (i + 1) + j // 2),
                               1.0 if j < 2 else RET_QK ** -0.5)
                for e in range(4):
                    act.wait_ge(sig("rav_done"), count(t, 4, 4 * i + e + 1))
                    nc.scalar.activation(r_o[:, e], ps[:, e], ACT.Copy).then_inc(sig("ro_done"), 1)
                if dense:
                    act.wait_ge(sig("rot_done"), count(t, 2, 2 * (i + 2)))
                    for j in range(4):
                        r_value(later(n, 4 + j), j, count(t, 4, 4 * (i + 1) + j - 1) if j >= 2 else None)
                for e in range(4):
                    act.wait_ge(sig("cen_done"), count(t, 4, 4 * i + e + 1))
                    nc.scalar.activation(r_sq[e], r_o[:, e], ACT.Square).then_inc(sig("rsq_done"), 1)
                gate = later(n, RET_QKV if dense else 0)
                for e in range(4):
                    if e == 2:
                        act.wait_ge(sig("rvar_done"), count(t, 4, 4 * i + 4))
                        nc.scalar.activation(std[:], ps[:, 5], ACT.Sqrt, bias=eps[:]).then_inc(sig("rstd_in"), 1)
                    split_hi(later(gate, e + 1))
                    nc.scalar.activation(r_g[:, e], product(later(gate, e)), ACT.Silu).then_inc(
                        bank_free[slot(later(gate, e))], 1)
                for e in range(4):
                    act.wait_ge(sig("ry_done"), count(t, 4, 4 * i + e + 1))
                    nc.scalar.activation(flat(y_hi[:, at(t, 4, 4 * i + e)]), r_o[:, e],
                                         ACT.Copy).then_inc(sig("yh_done"), 1)

            r_qkv(RUN_AT["ret"], None, 0)
            pairs(act, RUN_AT["ret"] + RET_QKV, 12 * (RET_HEADS - 1), lambda n, t: r_head(n, t, 0), step=12)
            r_head(RUN_AT["ret_out"] - RET_G, None, RET_HEADS - 1, dense=False)
            ahead(RUN_AT["ret_out"], 2 * DC)
            norm(N_MLP1)
            mlp(RUN_AT["mlp1"], HIDDEN // P)
            norm(N_FINAL)
            norm(N_FFN1)
            ffn(RUN_AT["ffn1"], 2 * HIDDEN // P)
            norm(N_MIX)

            def mix_two(n, t):
                for i in range(2):
                    split_hi(later(n, i + 1))
                    move(later(n, i), flat(pj[:, at(t, 2, i)]))

            pairs(act, RUN_AT["mix"], MIX_BLOCKS - 1, mix_two)
            split_hi(RUN_AT["proj"])
            move(RUN_AT["proj"] - 1, pj[:, MIX_BLOCKS - 1])

            act.wait_ge(sig("vt_mix"), 1)
            nc.scalar.activation(a_v[:].rearrange("p b f -> p (b f)"), ps[:, 0], ACT.Copy).then_inc(sig("vt_moved"), 1)
            for c in range(4):
                act.wait_ge(sig("vt_mix"), 2 + c)
                nc.scalar.activation(m_v[:, :, c * P:(c + 1) * P],
                                     ps[:, 1 + c].rearrange("p (b f) -> p b f", b=TB), ACT.Copy).then_inc(sig("vt_moved"), 1)

            for j, m in enumerate(HEAD_NORMED):
                if j >= 2:
                    act.wait_ge(sig("hms_done"), j - 1)
                nc.scalar.activation(n_sq[:, j % 2], pj[:, m], ACT.Square).then_inc(sig("hsq_done"), 1)
                act.wait_ge(sig("hms_done"), j + 1)
                if j >= 2:
                    act.wait_ge(sig("hr_done"), j - 1)
                nc.scalar.activation(n_std[:, j % 2], ps[:, j % 2], ACT.Sqrt, bias=eps[:]).then_inc(sig("hstd_done"), 1)

            for c in range(4):
                act.wait_ge(sig("conv_done"), c + 1)
                nc.scalar.activation(m_xc[:, c], m_xc[:, c], ACT.Silu).then_inc(sig("xc_done"), 1)
            act.wait_ge(sig("hr_done"), len(HEAD_NORMED))
            gate = pj[:, MIX_GATES]
            nc.scalar.activation(g_li[:], gate[GATE_I:GATE_I + ML_HEADS], ACT.Identity,
                                 bias=col("b_i", rows=ML_HEADS)).then_inc(sig("gate_done"), 1)
            nc.scalar.activation(g_lf[:], gate[GATE_F:GATE_F + ML_HEADS], ACT.Identity,
                                 bias=col("b_f", rows=ML_HEADS)).then_inc(sig("gate_done"), 1)
            act.wait_ge(sig("gabs_done"), 1)
            nc.scalar.activation(g_sum[:], g_sum[:], ACT.Exp, scale=-1.0).then_inc(sig("gexp_done"), 1)
            act.wait_ge(sig("gexp_done"), 1)
            nc.scalar.activation(g_sum[:], g_sum[:], ACT.Ln, bias=1.0).then_inc(sig("gexp_done"), 1)
            act.wait_ge(sig("ma_in"), 1)
            nc.scalar.activation(m_a[:], ps[:, 0, 0:TB * ML_HEADS].rearrange("p (b f) -> p b f", b=TB),
                                 ACT.Copy).then_inc(sig("ma_done"), 1)
            act.wait_ge(sig("ma_done"), 1)
            for hd in range(ML_HEADS):
                act.wait_ge(sig("mqk_done"), hd + 1)
                nc.scalar.activation(m_q[:], ps[0:ML_QK, 1], ACT.Copy, scale=ML_QK ** -0.5).then_inc(sig("mq_moved"), 1)
                nc.scalar.activation(m_k[:], ps[0:ML_QK, 2], ACT.Copy).then_inc(sig("mq_moved"), 1)
                act.wait_ge(sig("mmax_done"), hd + 1)
                for kb in range(TB):
                    nc.scalar.activation(m_w[:, S_AT[kb]:S_AT[kb] + P], ps[:, 4, kb * P:(kb + 1) * P], ACT.Exp,
                                         scale=-1.0, bias=m_a[:, kb, hd:hd + 1]).then_inc(sig("mexp_done"), 1)
                for kb in range(TB - 1):
                    nc.scalar.activation(m_w[:, S_AT[kb] + P:S_AT[kb] + seen_by(kb)], ps[:, 3, (kb + 1) * P:T],
                                         ACT.Exp, scale=-1.0, bias=m_a[:, kb, hd:hd + 1]).then_inc(sig("mexp_done"), 1)
                nc.scalar.activation(xn[:, 0], ps[:, 5], ACT.Exp, scale=-1.0).then_inc(sig("mexp_done"), 1)
                nc.scalar.activation(m_so[:], pj[:, MIX_MO + hd], ACT.Sigmoid).then_inc(sig("mso_done"), 1)
                act.wait_ge(sig("mh_done"), 3 * hd + 1)
                nc.scalar.activation(xn[:, 1], m_h[:], ACT.Square).then_inc(sig("msq_done"), 1)
                act.wait_ge(sig("mvar_done"), hd + 1)
                nc.scalar.activation(std[:], ps[:, 0], ACT.Sqrt, bias=eps[:]).then_inc(sig("mstd_done"), 1)
                act.wait_ge(sig("mh_done"), 3 * hd + 3)
                nc.scalar.activation(yb_hi[:, hd], m_h[:], ACT.Copy).then_inc(sig("yb_hi_done"), 1)

            act.wait_ge(sig("yb_lo_done"), ML_HEADS)
            for j in range(3 * IDX_HEADS):
                seen = (1 + j // IDX_HEADS + 1) * P
                act.wait_ge(sig("ilog_done"), j + 1)
                if j >= 2:
                    act.wait_ge(sig("iacc_done"), j - 1)
                nc.scalar.activation(rr[:, j % 2, 0:seen], ps[:, j % 2, 0:seen], ACT.Relu).then_inc(sig("irelu_done"), 1)
            def att_weights(j):
                tb = j // 2 % TB
                seen = (tb + 1) * P
                act.wait_ge(sig("amax_done"), j + 1)
                nc.scalar.activation(s_m[:, j % 2, 0:seen], s_m[:, j % 2, 0:seen], ACT.Exp, scale=ATT_DIM ** -0.5,
                                     bias=stat[:, 1, j:j + 1], accum_out=stat[:, 2, j:j + 1]).then_inc(sig("aexp_done"), 1)

            def att_turned(j):
                tb = j // 2 % TB
                seen = (tb + 1) * P
                act.wait_ge(sig("aturn_done"), j + 1)
                if j >= 2:
                    act.wait_ge(sig("apv_done"), j - 1)
                nc.scalar.activation(rr[:, j % 2, 0:seen], ps[:, 2 + j % 2, 0:seen], ACT.Copy).then_inc(sig("pt_done"), 1)

            n_att = ATT_HEADS * TB
            for j in range(n_att + 1):
                if j < n_att:
                    att_weights(j)
                if j >= 1:
                    att_turned(j - 1)
                    if (j - 1) % 8 == 7:
                        c = (j - 1) // 8
                        act.wait_ge(sig("apv_done"), j)
                        nc.scalar.activation(ya_hi[:, c], ps[:, 4 + c % 2], ACT.Copy).then_inc(sig("ya_hi_done"), 1)

            def merge(n, m):
                split_hi(n + 1)
                if m:
                    act.wait_ge(sig("mg_lo_done"), m)
                nc.scalar.activation(xn[:, 0], product(n), ACT.Sigmoid).then_inc(bank_free[slot(n)], 1)
                split_hi(n + 2)
                nc.scalar.activation(xn[:, 1], product(n + 1), ACT.Sigmoid).then_inc(bank_free[slot(n + 1)], 1)
                split_hi(n + 3)
                act.wait_ge(sig("mg_done"), m + 1)
                nc.scalar.activation(mg_hi[:, m], u_sum[:], ACT.Copy).then_inc(sig("mg_hi_done"), 1)

            for m in range(DC):
                merge(RUN_AT["proj"] + 3 * m, m)
            ahead(RUN_AT["w_out"], DC)
            norm(N_FFN2)
            ffn(RUN_AT["ffn2"], 2 * HIDDEN // P + D_FF // P)
            for i in range(2 * TB):
                act.wait_ge(sig("out_turned"), i + 1)
                nc.scalar.activation(x_tok[:, i // 2, (i % 2) * T:(i % 2 + 1) * T], ps[:, i % 4], ACT.Copy).then_inc(
                    sig("out_ready"), 1)

        @block.vector
        def _(dve):
            dve.sem_inc(lo_done, 2)
            dve.sem_inc(bank_free[0], 1)
            dve.sem_inc(bank_free[1], 1)

            def split_lo(n):
                if place_of(n)[1] is None and number(n) >= N_BLOCKS:
                    return
                dve.wait_ge(hi_done, number(n, 1))
                nc.vector.tensor_tensor(w_lo[:, slot(n)], raw[:, slot(n)], w_hi[:, slot(n)].bitcast(F32),
                                        ALU.subtract).then_inc(lo_done, 1)

            def product(n):
                dve.wait_ge(mm_done, number(n, 3))
                return ps[:, GEMM_BANK + slot(n)]

            def count(t, scale, plus):
                return plus if t is None else t * scale + plus

            split_norms = [k for k in range(len(NORMS)) if k != N_FINAL]

            def norm(k):
                name, _ = NORMS[k]
                dve.wait_ge(sig("std_done"), k + 1)
                nc.vector.reciprocal(rstd[:], std[:]).then_inc(sig("rstd_done"), 1)
                dve.wait_ge(sig("rstd_done"), k + 1)
                if k == N_FINAL:
                    for c in range(DC):
                        nc.vector.scalar_tensor_tensor(out=h[:, c], in0=h[:, c], scalar=col(name, c), in1=rstd[:],
                                                       op0=ALU.mult, op1=ALU.mult).then_inc(sig("final_done"), 1)
                    return
                nx = split_norms.index(k)

                def low(c):
                    dve.wait_ge(sig("xh_done"), nx * DC + c + 1)
                    nc.vector.tensor_tensor(x_lo[:, c], xn[:, c % 2], x_hi[:, c].bitcast(F32),
                                            ALU.subtract).then_inc(sig("xl_done"), 1)

                for c in range(DC):
                    if c >= 2:
                        low(c - 2)
                        dve.wait_ge(sig("xl_done"), nx * DC + c - 1)
                    if c == 0 and k == N_FFN1:
                        dve.wait_ge(sig("final_done"), DC)
                    nc.vector.scalar_tensor_tensor(out=xn[:, c % 2], in0=h[:, c], scalar=col(name, c), in1=rstd[:],
                                                   op0=ALU.mult, op1=ALU.mult).then_inc(sig("xn_done"), 1)
                    dve.wait_ge(sig("xn_done"), nx * DC + c + 1)
                low(DC - 2)
                low(DC - 1)

            for c in range(DC):
                dve.wait_ge(sig("x_turned"), c + 1)
                nc.vector.tensor_copy(h[:, c], ps[:, c % 4]).then_inc(sig("h_in"), 1)
            dve.wait_ge(sig("h_in"), DC)
            dve.wait_ge(sig("tables_in"), 32)
            split_lo(0)
            norm(N_MIX0)

            def sb_values(p):
                dve.wait_ge(sig("sbvt_done"), p)
                nc.vector.tensor_copy(sb_vt[:].rearrange("p b f -> p (b f)"), ps[:, 4]).then_inc(sig("sbv_done"), 1)

            for which in range(3):
                split_lo(which + 1)
            sb_values(1)

            def sb_pair(n, t, pc, step, dense=True):
                p = pc if t is None else t * step + pc
                if dense:
                    split_lo(later(n, 1))
                for z in range(Z_BANKS):
                    dve.wait_ge(sig("z_done"), p + 1)
                    nc.vector.tensor_copy(z_sp[:, z], ps[:, z]).then_inc(sig("zc_done"), 1)
                    dve.wait_ge(sig("zc_done"), p * Z_BANKS + (z + 1))
                    nc.vector.scalar_tensor_tensor(out=z_ex[:, z], in0=z_sp[:, z], scalar=-1.0, in1=z_sp[:, z],
                                                   op0=ALU.mult, op1=ALU.max).then_inc(sig("abs_done"), 1)
                if dense:
                    split_lo(later(n, 2))
                for z in range(Z_BANKS):
                    dve.wait_ge(sig("ln_done"), p * Z_BANKS + (z + 1))
                    nc.vector.scalar_tensor_tensor(out=z_sp[:, z], in0=z_sp[:, z], scalar=0.0, in1=z_ex[:, z],
                                                   op0=ALU.max, op1=ALU.add).then_inc(sig("sp_done"), 1)
                if dense:
                    split_lo(later(n, 3))
                dve.wait_ge(sig("oh_done"), p + 1)
                nc.vector.tensor_tensor(flat(o_lo[:, at(t, step, pc)]), ps[:, 5],
                                        flat(o_hi[:, at(t, step, pc)]).bitcast(F32), ALU.subtract).then_inc(sig("ol_done"), 1)
                if dense:
                    sb_values(p + 2)

            def sb_two(n, t):
                sb_pair(n, t, 0, 2)
                sb_pair(later(n, 3), t, 1, 2)

            pairs(dve, 3, 6 * 3, sb_two, step=6)
            sb_pair(3 * 7, None, 6, 0)
            sb_pair(None, None, 7, 0, dense=False)

            def residual(first, blocks, scale=1.0):
                def two(n, t):
                    for i in range(2):
                        split_lo(later(n, i + 1))
                        chunk = flat(h[:, at(t, 2, i)])
                        nc.vector.scalar_tensor_tensor(out=chunk, in0=product(later(n, i)), scalar=scale, in1=chunk,
                                                       op0=ALU.mult, op1=ALU.add).then_inc(bank_free[slot(later(n, i))], 1)

                def last_two(n, t):
                    for i in range(2):
                        split_lo(n + i + 1)
                        chunk = h[:, blocks - 2 + i]
                        nc.vector.scalar_tensor_tensor(out=chunk, in0=product(n + i), scalar=scale, in1=chunk,
                                                       op0=ALU.mult, op1=ALU.add).then_inc(bank_free[slot(n + i)], 1)

                if first + blocks == N_BLOCKS:
                    pairs(dve, first, blocks - 2, two)
                    last_two(N_BLOCKS - 2, None)
                else:
                    pairs(dve, first, blocks, two)

            residual(RUN_AT["sb_out"], DC)
            norm(N_MLP0)

            def hidden_lo(t, scale, plus, done, group):
                dve.wait_ge(sig("uh_done"), done)
                nc.vector.tensor_tensor(flat(u_lo[:, group % 2, at(t, scale, plus)]), u[:, plus],
                                        flat(u_hi[:, group % 2, at(t, scale, plus)]).bitcast(F32),
                                        ALU.subtract).then_inc(sig("ul_done"), 1)

            def mlp(first, chunks_before):
                def up(n, t, group, before):
                    for i in range(2):
                        m = later(n, i)
                        split_lo(later(n, i + 1))
                        dve.wait_ge(bank_free[slot(m)], turn(m, 2))
                        nc.vector.tensor_tensor(u[:, i], u_act[:], u_act[:], ALU.mult).then_inc(sig("u_done"), 1)
                        hidden_lo(t, 2, i, count(t, 2, before + i + 1), group)
                groups(MLP_GROUPS, first, chunks_before, 1, up, 1.0)

            def ffn(first, chunks_before):
                def up(n, t, group, before):
                    split_lo(later(n, 1))
                    split_lo(later(n, 2))
                    dve.wait_ge(bank_free[slot(n)], turn(n, 2))
                    m = later(n, 1)
                    dve.wait_ge(sig("ul_done"), count(t, 1, before))
                    nc.vector.tensor_tensor(u[:, 0], product(m), u_act[:], ALU.mult).then_inc(sig("u_done"), 1)
                    dve.wait_ge(sig("u_done"), count(t, 1, before + 1))
                    dve.sem_inc(bank_free[slot(m)], 1)
                    hidden_lo(t, 1, 0, count(t, 1, before + 1), group)
                groups(FFN_GROUPS, first, chunks_before, 2, up, 0.5)

            def groups(sizes, first, chunks_before, per_chunk, up, scale):
                n = first
                for g in range(len(sizes) + 1):
                    if g < len(sizes):
                        before = chunks_before + sum(sizes[:g])
                        pairs(dve, n, sizes[g] * per_chunk, lambda m, t: up(m, t, g, before))
                        n += sizes[g] * per_chunk
                    if g >= 1:
                        residual(n, DC, scale)
                        n += DC

            mlp(RUN_AT["mlp0"], 0)
            norm(N_MIX1)

            cos, sin = tab_ret[:, 0], tab_ret[:, 1]

            def step(name, made_at):
                dve.wait_ge(sig(name), made_at)

            def rotate(n, dst, t, i):
                dve.wait_ge(bank_free[slot(n)], turn(n, 2))
                if t is not None or i:
                    step("rot_done", count(t, 2, i))
                first, second = r_x[:, 0], r_x[:, 1]
                for half, (a, b, op) in enumerate(((cos, sin, ALU.subtract), (sin, cos, ALU.add))):
                    if half:
                        step("rhalf_done", count(t, 2, i + 1))
                    nc.vector.tensor_tensor(r_t[:, 0], first, a, ALU.mult).then_inc(sig("rt_done"), 1)
                    nc.vector.tensor_tensor(r_t[:, 1], second, b, ALU.mult).then_inc(sig("rt_done"), 1)
                    step("rt_done", count(t, 8, 4 * i + 2 * half + 2))
                    last = nc.vector.tensor_tensor(dst[:, half], r_t[:, 0], r_t[:, 1], op)
                    last.then_inc(sig("rot_done") if half else sig("rhalf_done"), 1)

            def r_values(t, i, j):
                dve.wait_ge(sig("rvt_done"), count(t, 4, 4 * i + j + 1))
                nc.vector.tensor_copy(r_v[:, :, j * P:(j + 1) * P],
                                      ps[:, 4].rearrange("p (b f) -> p b f", b=TB)).then_inc(sig("rv_done"), 1)

            def r_head(n, t, i, dense=True):
                for kb in range(TB):
                    dve.wait_ge(sig("rs_done"), count(t, 1, i + 1))
                    nc.vector.tensor_tensor(r_p[:, S_AT[kb]:S_AT[kb] + seen_by(kb)], s_flat[:, S_AT[kb]:S_AT[kb] + seen_by(kb)],
                                            flat(tab_ret[:, at(t, 1, 2 + i), 0:seen_by(kb)]), ALU.mult).then_inc(sig("rp_done"), 1)
                if dense:
                    for j in range(2):
                        split_lo(later(n, 2 * j + 1))
                        split_lo(later(n, 2 * j + 2))
                        rotate(later(n, 2 * j + 1), (r_q, r_k)[j], t, 2 * (i + 1) + j)
                    for j in range(4):
                        split_lo(later(n, 4 + j + 1))
                        if j >= 2:
                            r_values(t, i + 1, j - 2)
                    r_values(t, i + 1, 2)
                gate = later(n, RET_QKV if dense else 0)
                for e in range(4):
                    dve.wait_ge(sig("rmu_done"), count(t, 1, i + 1))
                    nc.vector.tensor_tensor(r_o[:, e], r_o[:, e], ps[:, 5], ALU.subtract).then_inc(sig("cen_done"), 1)
                split_lo(later(gate, 1))
                if dense:
                    r_values(t, i + 1, 3)
                split_lo(later(gate, 2))
                dve.wait_ge(sig("rstd_in"), count(t, 1, i + 1))
                nc.vector.reciprocal(rstd[:], std[:]).then_inc(sig("rrstd_done"), 1)
                split_lo(later(gate, 3))
                split_lo(later(gate, 4))
                step("rrstd_done", count(t, 1, i + 1))
                for e in range(4):
                    nc.vector.tensor_tensor(r_o[:, e], r_o[:, e], rstd[:], ALU.mult).then_inc(sig("rn_done"), 1)
                for e in range(4):
                    step("rn_done", count(t, 4, 4 * i + e + 1))
                    m = later(gate, e)
                    dve.wait_ge(bank_free[slot(m)], turn(m, 2))
                    nc.vector.tensor_tensor(r_o[:, e], r_o[:, e], r_g[:, e], ALU.mult).then_inc(sig("ry_done"), 1)
                for e in range(4):
                    dve.wait_ge(sig("yh_done"), count(t, 4, 4 * i + e + 1))
                    nc.vector.tensor_tensor(flat(y_lo[:, at(t, 4, 4 * i + e)]), r_o[:, e],
                                            flat(y_hi[:, at(t, 4, 4 * i + e)]).bitcast(F32), ALU.subtract).then_inc(sig("yl_done"), 1)

            s_flat = ps[:, 0:3].rearrange("p a b -> p (a b)")
            dve.wait_ge(sig("tables_ret_in"), 16)
            first = RUN_AT["ret"]
            for j in range(2):
                split_lo(first + 2 * j + 1)
                split_lo(first + 2 * j + 2)
                rotate(first + 2 * j + 1, (r_q, r_k)[j], None, j)
            for j in range(4):
                split_lo(first + 4 + j + 1)
                if j >= 2:
                    r_values(None, 0, j - 2)
            r_values(None, 0, 2)
            r_values(None, 0, 3)
            pairs(dve, first + RET_QKV, 12 * (RET_HEADS - 1), lambda n, t: r_head(n, t, 0), step=12)
            r_head(RUN_AT["ret_out"] - RET_G, None, RET_HEADS - 1, dense=False)
            residual(RUN_AT["ret_out"], DC)
            residual(RUN_AT["ret_out"] + DC, DC)
            norm(N_MLP1)
            mlp(RUN_AT["mlp1"], HIDDEN // P)
            norm(N_FINAL)
            norm(N_FFN1)
            ffn(RUN_AT["ffn1"], 2 * HIDDEN // P)
            norm(N_MIX)

            pairs(dve, RUN_AT["mix"], MIX_BLOCKS - 1, lambda n, t: (split_lo(later(n, 1)), split_lo(later(n, 2))))
            split_lo(RUN_AT["proj"])
            dve.wait_ge(sig("vt_mix"), 6)
            nc.vector.tensor_scalar(iw[:], ps[:, 5].rearrange("p (b f) -> p b f", b=TB)[:, :, GATE_IW:GATE_IW + IDX_HEADS],
                                    IDX_DIM ** -0.5 * IDX_HEADS ** -0.5, None, ALU.mult).then_inc(sig("iw_done"), 1)
            for j, (m, gain) in enumerate(HEAD_NORMED.items()):
                dve.wait_ge(sig("hstd_done"), j + 1)
                nc.vector.reciprocal(n_r[:, j % 2], n_std[:, j % 2]).then_inc(sig("hr_done"), 1)
                step("hr_done", j + 1)
                nc.vector.scalar_tensor_tensor(out=pj[:, m], in0=pj[:, m], scalar=col(gain), in1=n_r[:, j % 2],
                                               op0=ALU.mult, op1=ALU.mult).then_inc(sig("hn_done"), 1)

            def tap(c, i):
                return col("conv_w", c * CONV + i)

            steps = 0
            for c in range(4):
                mx, xc = pj[:, MIX_MX + c], m_xc[:, c]
                nc.vector.tensor_scalar(xc, mx, tap(c, CONV - 1), col("conv_b", c), ALU.mult, ALU.add).then_inc(sig("tap_done"), 1)
                for back in range(1, CONV):
                    steps += 1
                    step("tap_done", steps)
                    nc.vector.scalar_tensor_tensor(out=xc[:, back:T], in0=mx[:, 0:T - back], scalar=tap(c, CONV - 1 - back),
                                                   in1=xc[:, back:T], op0=ALU.mult, op1=ALU.add).then_inc(
                        sig("tap_done") if back < CONV - 1 else sig("conv_done"), 1)

            dve.wait_ge(sig("gate_done"), 2)
            nc.vector.scalar_tensor_tensor(out=g_sum[:], in0=g_lf[:], scalar=-1.0, in1=g_lf[:], op0=ALU.mult,
                                           op1=ALU.max).then_inc(sig("gabs_done"), 1)
            nc.vector.memset(g_max[:], 1.0).then_inc(sig("gone_done"), 1)
            dve.wait_ge(sig("gexp_done"), 2)
            nc.vector.scalar_tensor_tensor(out=g_lf[:], in0=g_lf[:], scalar=0.0, in1=g_sum[:], op0=ALU.min,
                                           op1=ALU.subtract).then_inc(sig("grow_done"), 1)
            step("grow_done", 1)
            step("gone_done", 1)
            nc.vector.tensor_tensor_scan(g_sum[:], g_max[:], g_lf[:], 0.0, ALU.mult, ALU.add).then_inc(sig("grow_done"), 1)
            step("grow_done", 2)
            nc.vector.tensor_tensor(g_a[:], g_li[:], g_sum[:], ALU.subtract).then_inc(sig("grow_done"), 1)
            step("grow_done", 3)
            nc.vector.tensor_tensor_scan(g_max[:], g_a[:], g_a[:], 0.0, ALU.max, ALU.max).then_inc(sig("grow_done"), 1)
            step("grow_done", 4)
            nc.vector.tensor_tensor(g_lf[:], g_max[:], g_sum[:], ALU.add).then_inc(sig("grow_done"), 1)

            for hd in range(ML_HEADS):
                dve.wait_ge(sig("mexp_done"), 8 * (hd + 1))
                dve.wait_ge(sig("mscore_done"), hd + 1)
                for kb in range(TB):
                    part = slice(S_AT[kb], S_AT[kb] + seen_by(kb))
                    nc.vector.tensor_tensor(m_w[:, part], s_flat[:, part], m_w[:, part], ALU.mult).then_inc(sig("mw_done"), 1)
                dve.wait_ge(sig("mnum_done"), hd + 1)
                nc.vector.scalar_tensor_tensor(out=rstd[:], in0=ps[:, 4], scalar=-1.0, in1=xn[:, 0], op0=ALU.mult,
                                               op1=ALU.max).then_inc(sig("mden_done"), 1)
                step("mden_done", 4 * hd + 1)
                nc.vector.tensor_tensor(rstd[:], ps[:, 4], rstd[:], ALU.max).then_inc(sig("mden_done"), 1)
                step("mden_done", 4 * hd + 2)
                nc.vector.reciprocal(rstd[:], rstd[:]).then_inc(sig("mden_done"), 1)
                step("mden_done", 4 * hd + 3)
                nc.vector.tensor_tensor(m_h[:], ps[:, 3], rstd[:], ALU.mult).then_inc(sig("mh_done"), 1)
                dve.wait_ge(sig("mstd_done"), hd + 1)
                step("mh_done", 3 * hd + 1)
                nc.vector.reciprocal(rstd[:], std[:]).then_inc(sig("mden_done"), 1)
                step("mden_done", 4 * hd + 4)
                nc.vector.scalar_tensor_tensor(out=m_h[:], in0=m_h[:], scalar=col("head_norm", hd), in1=rstd[:],
                                               op0=ALU.mult, op1=ALU.mult).then_inc(sig("mh_done"), 1)
                step("mh_done", 3 * hd + 2)
                dve.wait_ge(sig("mso_done"), hd + 1)
                nc.vector.tensor_tensor(m_h[:], m_h[:], m_so[:], ALU.mult).then_inc(sig("mh_done"), 1)
                dve.wait_ge(sig("yb_hi_done"), hd + 1)
                nc.vector.tensor_tensor(yb_lo[:, hd], m_h[:], yb_hi[:, hd].bitcast(F32), ALU.subtract).then_inc(sig("yb_lo_done"), 1)

            step("yb_lo_done", ML_HEADS)
            step("iw_done", 1)
            nc.vector.memset(neg[:, 0:P], 0.0).then_inc(sig("neg_done"), 1)
            step("neg_done", 1)
            nc.vector.memset(neg[0:CHUNK, CHUNK:P], -BIG).then_inc(sig("neg_done"), 1)
            for tb in range(1, TB):
                seen = (tb + 1) * P
                row = score[:, 0:seen]
                for hd in range(IDX_HEADS):
                    j = (tb - 1) * IDX_HEADS + hd
                    dve.wait_ge(sig("irelu_done"), j + 1)
                    weight = iw[:, tb, hd:hd + 1]
                    if hd == 0:
                        nc.vector.tensor_scalar(row, rr[:, j % 2, 0:seen], weight, None, ALU.mult).then_inc(sig("iacc_done"), 1)
                    else:
                        step("iacc_done", j)
                        nc.vector.scalar_tensor_tensor(out=row, in0=rr[:, j % 2, 0:seen], scalar=weight, in1=row,
                                                       op0=ALU.mult, op1=ALU.add).then_inc(sig("iacc_done"), 1)
                step("iacc_done", tb * IDX_HEADS)
                nc.vector.memset(score[0:CHUNK, seen - CHUNK:seen], OUT_OF_REACH).then_inc(sig("cut_done"), 1)
                step("cut_done", tb)

                def take(t):
                    base = (tb - 1) * (TOPK // 8)
                    nc.vector.max(best[:], row).then_inc(sig("best_done"), 1)
                    step("best_done", t + (base + 1))
                    nc.vector.match_replace(row, best[:], row, TAKEN).then_inc(sig("taken_done"), 1)
                    step("taken_done", t + (base + 1))

                for t in range(TOPK // 8):
                    take(t)
                nc.vector.tensor_scalar(neg[:, NEG_AT[tb]:NEG_AT[tb] + seen], row, OUT_OF_REACH * 2, -BIG,
                                        ALU.is_gt, ALU.mult).then_inc(sig("neg_done"), 1)
                step("neg_done", tb + 2)

            def att_max(j):
                tb = j // 2 % TB
                seen = (tb + 1) * P
                dve.wait_ge(sig("as_done"), j + 1)
                if j >= 2:
                    dve.wait_ge(sig("aturn_done"), j - 1)
                nc.vector.tensor_tensor_reduce(out=s_m[:, j % 2, 0:seen], in0=ps[:, j % 2, 0:seen],
                                               in1=neg[:, NEG_AT[tb]:NEG_AT[tb] + seen], scale=1.0, scalar=TAKEN,
                                               op0=ALU.add, op1=ALU.max, accum_out=stat[:, 0, j:j + 1]).then_inc(sig("arow_done"), 1)
                step("arow_done", j + 1)
                nc.vector.tensor_scalar(stat[:, 1, j:j + 1], stat[:, 0, j:j + 1], -(ATT_DIM ** -0.5), None,
                                        ALU.mult).then_inc(sig("amax_done"), 1)

            def att_norm(j):
                seen = (j // 2 % TB + 1) * P
                dve.wait_ge(sig("aexp_done"), j + 1)
                nc.vector.reciprocal(stat[:, 3, j:j + 1], stat[:, 2, j:j + 1]).then_inc(sig("ainv_done"), 1)
                step("ainv_done", j + 1)
                nc.vector.tensor_scalar(s_m[:, j % 2, 0:seen], s_m[:, j % 2, 0:seen], stat[:, 3, j:j + 1], None,
                                        ALU.mult).then_inc(sig("anorm_done"), 1)

            n_att = ATT_HEADS * TB
            for j in range(n_att + 1):
                if j < n_att:
                    att_max(j)
                if j >= 1:
                    att_norm(j - 1)
                if j >= 9 and (j - 2) % 8 == 7 or j == n_att:
                    c = (j - 2) // 8 if j < n_att else 3
                    dve.wait_ge(sig("ya_hi_done"), c + 1)
                    nc.vector.tensor_tensor(ya_lo[:, c], ps[:, 4 + c % 2], ya_hi[:, c].bitcast(F32),
                                            ALU.subtract).then_inc(sig("ya_lo_done"), 1)

            def merge(n, m):
                split_lo(n + 1)
                split_lo(n + 2)
                dve.wait_ge(bank_free[slot(n)], turn(n, 2))
                dve.wait_ge(bank_free[slot(n + 1)], turn(n + 1, 2))
                split_lo(n + 3)
                nc.vector.tensor_tensor(std[:], product(n + 2), xn[:, 0], ALU.mult).then_inc(bank_free[slot(n + 2)], 1)
                nc.vector.tensor_tensor(u_sum[:], ps[:, 5], xn[:, 1], ALU.mult).then_inc(sig("mgb_done"), 1)
                dve.wait_ge(bank_free[slot(n + 2)], turn(n + 2, 2))
                step("mgb_done", m + 1)
                nc.vector.tensor_tensor(u_sum[:], std[:], u_sum[:], ALU.add).then_inc(sig("mg_done"), 1)
                dve.wait_ge(sig("mg_hi_done"), m + 1)
                nc.vector.tensor_tensor(mg_lo[:, m], u_sum[:], mg_hi[:, m].bitcast(F32), ALU.subtract).then_inc(sig("mg_lo_done"), 1)

            for m in range(DC):
                merge(RUN_AT["proj"] + 3 * m, m)
            residual(RUN_AT["w_out"], DC)
            norm(N_FFN2)
            ffn(RUN_AT["ffn2"], 2 * HIDDEN // P + D_FF // P)

        @block.gpsimd
        def _(pool):
            for t, value in ((mean_d, 1 / D), (mean_v, 1 / RET_V), (one, 1.0), (neg_one, -1.0), (eps[:], EPS)):
                nc.gpsimd.memset(t, value).then_inc(sig("consts"), 1)

        @block.tensor
        def _(pe):
            pe.sem_inc(mm_done, 2)

            def dense(n, hi, lo, kc=KC):
                pe.wait_ge(lo_done, number(n, 3))
                pe.wait_ge(bank_free[slot(n)], turn(n, 1))
                s = slot(n)
                for k in range(kc):
                    for i, (w, x) in enumerate(((w_hi, hi), (w_hi, lo), (w_lo, hi))):
                        last = nc.tensor.matmul(ps[:, GEMM_BANK + s], w[:, s, k], x(k), start=(k == 0 and i == 0),
                                                stop=(k == kc - 1 and i == 2))
                last.then_inc(mm_done, 1)

            def count(t, scale, plus):
                return plus if t is None else t * scale + plus

            def of_x(n):
                dense(n, lambda k: x_hi[:, k], lambda k: x_lo[:, k])

            split_norms = [k for k in range(len(NORMS)) if k != N_FINAL]

            def norm(k, wait=True):
                for c in range(DC):
                    pe.wait_ge(sig("sq_done"), k * DC + c + 1)
                    last = nc.tensor.matmul(ps[:, 5], mean_d, squares[:, c], start=(c == 0), stop=(c == DC - 1))
                last.then_inc(sig("ms_done"), 1)
                if k != N_FINAL:
                    pe.wait_ge(sig("xl_done"), (split_norms.index(k) + 1) * DC)

            def turn_block(dst, src):
                return nc.tensor.transpose(dst, src, ident)

            pe.wait_ge(sig("x_in"), 16)
            pe.wait_ge(sig("tables_in"), 32)
            for c in range(DC):
                if c >= 4:
                    pe.wait_ge(sig("h_in"), c - 3)
                for b in range(TB):
                    last = turn_block(ps[:, c % 4, b * P:(b + 1) * P], x_tok[:, b, c * P:(c + 1) * P])
                last.then_inc(sig("x_turned"), 1)
            pe.wait_ge(sig("consts"), 5)
            norm(N_MIX0)

            z_flat = ps[:, 0:Z_BANKS].rearrange("p a b -> p (a b)")
            sp_flat = z_sp[:].rearrange("p a b -> p (a b)")
            a_flat = z_ex[:].rearrange("p a b -> p (a b)")

            def moved(n):
                pe.wait_ge(bank_free[slot(n)], turn(n, 2))

            def sb_turn(n):
                moved(n)
                for b in range(TB):
                    last = turn_block(ps[:, 4, b * P:(b + 1) * P], sb_v[:, b * P:(b + 1) * P])
                last.then_inc(sig("sbvt_done"), 1)

            def sb_scores(n, p):
                moved(later(n, 1))
                pe.wait_ge(sig("sbv_done"), p)
                for hd in range(2):
                    rows = slice(hd * SB_DIM, (hd + 1) * SB_DIM)
                    for kb in (2, 0, 1, 3) if hd == 0 else (0, 1, 3, 2):
                        c = Z_AT[hd, kb]
                        if hd == 1 and kb == 2:
                            pe.wait_ge(sig("z_shared_done"), p)
                        nc.tensor.matmul(z_flat[:, c:c + seen_by(kb)], sb_k[rows, kb * P:(kb + 1) * P],
                                         sb_q[rows, kb * P:T], start=(c % T == 0), stop=False, skip_group_check=True)
                        last = nc.tensor.matmul(z_flat[:, c:c + P], ident, strict, start=False, stop=False,
                                                skip_group_check=True)
                        if hd == 0 and kb == 2:
                            last.then_inc(sig("z_shared_done"), 1)
                last.then_inc(sig("z_done"), 1)

            def sb_sums(p):
                pe.wait_ge(sig("sp_done"), p)
                for hd in range(2):
                    for kb in range(TB):
                        for jb in range(kb, TB):
                            c = Z_AT[hd, kb] + (jb - kb) * P
                            src = Z_AT[hd, jb]
                            last = nc.tensor.matmul(z_flat[:, c:c + seen_by(jb)], neg_tri if jb == kb else neg_one,
                                                    sp_flat[:, src:src + seen_by(jb)], start=False, stop=(jb == TB - 1),
                                                    skip_group_check=True)
                last.then_inc(sig("cum_done"), 1)

            def sb_out(p):
                pe.wait_ge(sig("a_done"), p)
                for hd in range(2):
                    rows = slice(hd * SB_DIM, (hd + 1) * SB_DIM)
                    for kb in range(TB):
                        c = Z_AT[hd, kb]
                        last = nc.tensor.matmul(ps[rows, 5, kb * P:T], sb_vt[:, kb, rows], a_flat[:, c:c + seen_by(kb)],
                                                start=(kb == 0), stop=(kb == TB - 1), skip_group_check=True)
                last.then_inc(sig("av_done"), 1)

            for which in range(3):
                of_x(which)
            sb_turn(2)

            def sb_pair(n, t, pc, step, dense_=True):
                sb_scores(later(n, -3), count(t, step, pc + 1))
                if dense_:
                    of_x(n)
                    of_x(later(n, 1))
                sb_sums(count(t, step * Z_BANKS, (pc + 1) * Z_BANKS))
                if dense_:
                    of_x(later(n, 2))
                sb_out(count(t, step * Z_BANKS, (pc + 1) * Z_BANKS))
                if dense_:
                    sb_turn(later(n, 2))

            def sb_two(n, t):
                sb_pair(n, t, 0, 2)
                sb_pair(later(n, 3), t, 1, 2)

            pairs(pe, 3, 6 * 3, sb_two, step=6)
            sb_pair(3 * 7, None, 6, 0)
            sb_pair(3 * 8, None, 7, 0, dense_=False)

            def run(first, blocks, hi, lo, kc=KC):
                def two(n, _):
                    dense(n, hi, lo, kc)
                    dense(later(n, 1), hi, lo, kc)
                pairs(pe, first, blocks, two)

            pe.wait_ge(sig("ol_done"), DC)
            run(RUN_AT["sb_out"], DC, lambda k: o_hi[:, k], lambda k: o_lo[:, k])
            norm(N_MLP0)

            def groups(sizes, first, chunks_before, per_chunk):
                n = first
                for g in range(len(sizes) + 1):
                    if g < len(sizes):
                        run(n, sizes[g] * per_chunk, lambda k: x_hi[:, k], lambda k: x_lo[:, k])
                        n += sizes[g] * per_chunk
                    if g >= 1:
                        b = (g - 1) % 2
                        pe.wait_ge(sig("ul_done"), chunks_before + sum(sizes[:g]))
                        run(n, DC, lambda k: u_hi[:, b, k], lambda k: u_lo[:, b, k], sizes[g - 1])
                        n += DC

            groups(MLP_GROUPS, RUN_AT["mlp0"], 0, 1)
            norm(N_MIX1)

            s_flat = ps[:, 0:3].rearrange("p a b -> p (a b)")

            def r_turn(n, j):
                moved(n)
                for b in range(TB):
                    last = turn_block(ps[:, 4, b * P:(b + 1) * P], r_t[:, j % 2, b * P:(b + 1) * P])
                last.then_inc(sig("rvt_done"), 1)

            def r_head(n, t, i, dense_=True):
                pe.wait_ge(sig("rot_done"), count(t, 2, 2 * i + 2))
                for kb in (0, 1, 3, 2):
                    c = S_AT[kb]
                    for k in range(2):
                        last = nc.tensor.matmul(s_flat[:, c:c + seen_by(kb)], r_k[:, k, kb * P:(kb + 1) * P], r_q[:, k, kb * P:T],
                                                start=(c % T == 0 and k == 0), stop=(k == 1), skip_group_check=True)
                last.then_inc(sig("rs_done"), 1)
                if dense_:
                    for j in range(4):
                        of_x(later(n, j))
                pe.wait_ge(sig("rp_done"), count(t, 4, 4 * i + 4))
                pe.wait_ge(sig("rv_done"), count(t, 4, 4 * i + 4))
                for e in range(4):
                    for kb in range(TB):
                        c = S_AT[kb]
                        last = nc.tensor.matmul(ps[:, e, kb * P:T], r_v[:, kb, e * P:(e + 1) * P], r_p[:, c:c + seen_by(kb)],
                                                start=(kb == 0), stop=(kb == TB - 1))
                    last.then_inc(sig("rav_done"), 1)
                if dense_:
                    for j in range(4):
                        of_x(later(n, 4 + j))
                        if j >= 1:
                            if j >= 2:
                                pe.wait_ge(sig("rv_done"), count(t, 4, 4 * (i + 1) + j - 1))
                            r_turn(later(n, 4 + j - 1), j - 1)
                pe.wait_ge(sig("ro_done"), count(t, 4, 4 * i + 4))
                for e in range(4):
                    last = nc.tensor.matmul(ps[:, 5], mean_v, r_o[:, e], start=(e == 0), stop=(e == 3))
                last.then_inc(sig("rmu_done"), 1)
                gate = later(n, RET_QKV if dense_ else 0)
                of_x(gate)
                if dense_:
                    pe.wait_ge(sig("rv_done"), count(t, 4, 4 * (i + 1) + 3))
                    r_turn(later(n, 7), 3)
                of_x(later(gate, 1))
                pe.wait_ge(sig("cen_done"), count(t, 4, 4 * i + 4))
                for e in range(4):
                    pe.wait_ge(sig("rsq_done"), count(t, 4, 4 * i + e + 1))
                    nc.tensor.matmul(ps[:, 5], mean_v, r_sq[e], start=(e == 0), stop=(e == 3)).then_inc(sig("rvar_done"), 1)
                of_x(later(gate, 2))
                of_x(later(gate, 3))

            first = RUN_AT["ret"]
            for j in range(8):
                of_x(first + j)
                if j >= 5:
                    if j >= 6:
                        pe.wait_ge(sig("rv_done"), j - 5)
                    r_turn(first + j - 1, j - 5)
            pe.wait_ge(sig("rv_done"), 3)
            r_turn(first + 7, 3)
            pairs(pe, first + RET_QKV, 12 * (RET_HEADS - 1), lambda n, t: r_head(n, t, 0), step=12)
            r_head(RUN_AT["ret_out"] - RET_G, None, RET_HEADS - 1, dense_=False)
            pe.wait_ge(sig("yl_done"), 2 * DC)
            for half in range(2):
                run(RUN_AT["ret_out"] + half * DC, DC, lambda k: y_hi[:, half * DC + k], lambda k: y_lo[:, half * DC + k])
            norm(N_MLP1)
            groups(MLP_GROUPS, RUN_AT["mlp1"], HIDDEN // P, 1)
            norm(N_FINAL)
            norm(N_FFN1)
            groups(FFN_GROUPS, RUN_AT["ffn1"], 2 * HIDDEN // P, 2)
            norm(N_MIX)

            run(RUN_AT["mix"], MIX_BLOCKS - 1, lambda k: x_hi[:, k], lambda k: x_lo[:, k])
            of_x(RUN_AT["proj"] - 1)
            for i, m in enumerate((MIX_V, MIX_MV, MIX_MV + 1, MIX_MV + 2, MIX_MV + 3, MIX_GATES)):
                moved(RUN_AT["mix"] + m)
                for b in range(TB):
                    last = turn_block(ps[:, i, b * P:(b + 1) * P], pj[:, m, b * P:(b + 1) * P])
                last.then_inc(sig("vt_mix"), 1)
            moved(RUN_AT["proj"] - 2)
            moved(RUN_AT["proj"] - 1)
            pe.wait_ge(sig("vt_moved"), 5)
            pe.wait_ge(sig("iw_done"), 1)
            for j in range(len(HEAD_NORMED)):
                pe.wait_ge(sig("hsq_done"), j + 1)
                if j >= 2:
                    pe.wait_ge(sig("hstd_done"), j - 1)
                nc.tensor.matmul(ps[:, j % 2], head_mean, n_sq[:, j % 2], start=True, stop=True).then_inc(sig("hms_done"), 1)

            pe.wait_ge(sig("hn_done"), len(HEAD_NORMED))
            pe.wait_ge(sig("grow_done"), 5)
            pe.wait_ge(sig("tables_mix_in"), 16)
            for b in range(TB):
                last = nc.tensor.transpose(ps[:, 0, b * ML_HEADS:(b + 1) * ML_HEADS], g_a[:, b * P:(b + 1) * P],
                                           ident[0:ML_HEADS, 0:ML_HEADS])
            last.then_inc(sig("ma_in"), 1)
            pe.wait_ge(sig("ma_done"), 1)
            for hd in range(ML_HEADS):
                if hd:
                    pe.wait_ge(sig("mh_done"), 3 * hd)
                pe.wait_ge(sig("xc_done"), 4)
                for i in range(2):
                    c = PARAMS["w_mqk"][0] + (2 * hd + i) * ML_QK
                    last = nc.tensor.matmul(ps[0:ML_QK, 1 + i], prm[:, c:c + ML_QK], m_xc[:, hd], start=True, stop=True)
                last.then_inc(sig("mqk_done"), 1)
                pick = tab_mix[0:ML_HEADS, hd]
                nc.tensor.matmul(ps[:, 3], pick, g_max[:], start=True, stop=True)
                nc.tensor.matmul(ps[:, 4], pick, g_max[:], start=True, stop=True, skip_group_check=True)
                for kb in range(TB):
                    nc.tensor.matmul(ps[:, 4, kb * P:(kb + 1) * P], ident, later_keys, start=False, stop=True,
                                     skip_group_check=True)
                nc.tensor.matmul(ps[:, 5], pick, g_lf[:], start=True, stop=True).then_inc(sig("mmax_done"), 1)
                pe.wait_ge(sig("mq_moved"), 2 * hd + 2)
                for kb in (0, 1, 3, 2):
                    c = S_AT[kb]
                    last = nc.tensor.matmul(s_flat[:, c:c + seen_by(kb)], m_k[:, kb * P:(kb + 1) * P], m_q[:, kb * P:T],
                                            start=(c % T == 0), stop=True, skip_group_check=True)
                last.then_inc(sig("mscore_done"), 1)
                pe.wait_ge(sig("mw_done"), 4 * hd + 4)
                for bank, lhs in ((3, lambda kb: m_v[:, kb, hd * P:(hd + 1) * P]), (4, lambda kb: one)):
                    for kb in range(TB):
                        c = S_AT[kb]
                        last = nc.tensor.matmul(ps[:, bank, kb * P:T], lhs(kb), m_w[:, c:c + seen_by(kb)],
                                                start=(kb == 0), stop=(kb == TB - 1))
                last.then_inc(sig("mnum_done"), 1)
                pe.wait_ge(sig("msq_done"), hd + 1)
                nc.tensor.matmul(ps[:, 0], mean_h, xn[:, 1], start=True, stop=True).then_inc(sig("mvar_done"), 1)

            pe.wait_ge(sig("yb_lo_done"), ML_HEADS)
            for j in range(3 * IDX_HEADS):
                tb, hd = 1 + j // IDX_HEADS, j % IDX_HEADS
                rows = slice(hd % 2 * IDX_DIM, (hd % 2 + 1) * IDX_DIM)
                if j >= 2:
                    pe.wait_ge(sig("irelu_done"), j - 1)
                nc.tensor.matmul(ps[:, j % 2, 0:(tb + 1) * P], pj[rows, MIX_IQ + hd // 2, tb * P:(tb + 1) * P],
                                 pj[rows, MIX_IK, 0:(tb + 1) * P], start=True, stop=True).then_inc(sig("ilog_done"), 1)
            pe.wait_ge(sig("irelu_done"), 3 * IDX_HEADS)

            def att_scores(j):
                c, tb, hd = j // 8, j // 2 % TB, j % 2
                rows = slice(hd * ATT_DIM, (hd + 1) * ATT_DIM)
                if j >= 2:
                    pe.wait_ge(sig("amax_done"), j - 1)
                kv = (2 * c + hd) // (ATT_HEADS // ATT_KV)
                nc.tensor.matmul(ps[:, j % 2, 0:(tb + 1) * P], pj[rows, MIX_Q + c, tb * P:(tb + 1) * P],
                                 pj[rows, MIX_K + kv, 0:(tb + 1) * P], start=True, stop=True).then_inc(sig("as_done"), 1)

            def att_turn(j):
                tb = j // 2 % TB
                pe.wait_ge(sig("anorm_done"), j + 1)
                if j >= 2:
                    pe.wait_ge(sig("pt_done"), j - 1)
                for kb in range(tb + 1):
                    last = turn_block(ps[:, 2 + j % 2, kb * P:(kb + 1) * P], s_m[:, j % 2, kb * P:(kb + 1) * P])
                last.then_inc(sig("aturn_done"), 1)

            def att_out(j):
                c, tb, hd = j // 8, j // 2 % TB, j % 2
                kv = (2 * c + hd) // (ATT_HEADS // ATT_KV)
                pe.wait_ge(sig("pt_done"), j + 1)
                if c >= 2 and j % 8 == 0:
                    pe.wait_ge(sig("ya_lo_done"), c - 1)
                for kb in range(tb + 1):
                    last = nc.tensor.matmul(ps[hd * ATT_DIM:(hd + 1) * ATT_DIM, 4 + c % 2, tb * P:(tb + 1) * P],
                                            a_v[:, kb, kv * ATT_DIM:(kv + 1) * ATT_DIM], rr[:, j % 2, kb * P:(kb + 1) * P],
                                            start=(kb == 0), stop=(kb == tb), skip_group_check=True)
                last.then_inc(sig("apv_done"), 1)

            n_att = ATT_HEADS * TB
            for j in range(n_att + 2):
                if j < n_att:
                    att_scores(j)
                if 1 <= j <= n_att:
                    att_turn(j - 1)
                if j >= 2:
                    att_out(j - 2)

            pe.wait_ge(sig("ya_lo_done"), 4)
            for m in range(DC):
                n = RUN_AT["proj"] + 3 * m
                of_x(n)
                of_x(n + 1)
                pe.wait_ge(lo_done, number(n + 2, 3))
                pe.wait_ge(bank_free[slot(n + 2)], turn(n + 2, 1))
                if m:
                    pe.wait_ge(sig("mgb_done"), m)
                for bank, k0, hi, lo in ((GEMM_BANK + slot(n + 2), 0, ya_hi, ya_lo), (5, 4, yb_hi, yb_lo)):
                    for k in range(4):
                        for i, (w, x) in enumerate(((w_hi, hi), (w_hi, lo), (w_lo, hi))):
                            last = nc.tensor.matmul(ps[:, bank], w[:, slot(n + 2), k0 + k], x[:, k],
                                                    start=(k == 0 and i == 0), stop=(k == 3 and i == 2))
                last.then_inc(mm_done, 1)
            pe.wait_ge(sig("mg_lo_done"), DC)
            run(RUN_AT["w_out"], DC, lambda k: mg_hi[:, k], lambda k: mg_lo[:, k])
            norm(N_FFN2)
            groups(FFN_GROUPS, RUN_AT["ffn2"], 2 * HIDDEN // P + D_FF // P, 2)

            moved(N_BLOCKS - 2)
            moved(N_BLOCKS - 1)
            for i in range(2 * TB):
                if i >= 4:
                    pe.wait_ge(sig("out_ready"), i - 3)
                for q in range(4):
                    last = turn_block(ps[:, i % 4, q * P:(q + 1) * P], h[:, i % 2 * 4 + q, i // 2 * P:(i // 2 + 1) * P])
                last.then_inc(sig("out_turned"), 1)



def weight_block(w, rows, cols):
    out = np.zeros((KC, P, P), np.float32)
    part = w[rows, cols]
    out[:part.shape[0] // P] = part.reshape(-1, P, part.shape[1])
    return out


def weight_stream(a):
    blocks = []

    def take(w, c, row=0, chunks=KC):
        blocks.append(weight_block(w, slice(row * P, (row + chunks) * P), slice(c * P, (c + 1) * P)))

    sb_in = a["w_sb_in"][0]
    for p in range(DC):
        for which in range(3):
            take(sb_in, which * DC + p)
    for m in range(DC):
        take(a["w_sb_out"][0], m)

    def mlp(ups, down, sizes):
        for g in range(len(sizes) + 1):
            if g < len(sizes):
                for m in range(sum(sizes[:g]), sum(sizes[:g + 1])):
                    for up in ups:
                        take(up, m)
            if g >= 1:
                for m in range(DC):
                    take(down, m, sum(sizes[:g - 1]), sizes[g - 1])

    mlp([a["w_mlp_up"][0]], a["w_mlp_down"][0], MLP_GROUPS)
    ret = a["w_ret_in"][0]

    def qkv(hd):
        for c in (2 * hd, 2 * hd + 1, DC + 2 * hd, DC + 2 * hd + 1):
            take(ret, c)
        for e in range(4):
            take(ret, 2 * DC + 4 * hd + e)

    qkv(0)
    for hd in range(RET_HEADS):
        if hd + 1 < RET_HEADS:
            qkv(hd + 1)
        for e in range(4):
            take(ret, 4 * DC + 4 * hd + e)
    for half in range(2):
        for m in range(DC):
            take(a["w_ret_out"][0], m, half * DC)
    mlp([a["w_mlp_up"][1]], a["w_mlp_down"][1], MLP_GROUPS)
    mlp([a["ffn1_w_gate_2"][0], a["ffn1_w_up_2"][0]], a["ffn1_w_down_2"][0], FFN_GROUPS)

    w_in = a["w_in_2"][0]
    widths = (512, 128, 128, 512, 64, 8, 512, 512, 4, 4, 512, 1024, 1024)
    aq, ak, av, iq, ik, iw, mx, mv, mi, mf, mo, ga, gb = np.cumsum((0,) + widths[:-1])

    def pick(cols):
        blocks.append(w_in[:, np.asarray(cols)].reshape(KC, P, P))

    def span(start, n=P):
        return list(range(start, start + n))

    for g in range(ATT_KV):
        pick(span(ak + g * ATT_DIM, ATT_DIM) * 2)
    for c in range(4):
        pick(span(aq + c * P))
    pick(span(av))
    pick(span(ik, IDX_DIM) * 2)
    for c in range(4):
        pick(span(iq + c * P))
    pick(span(iw, 32) + span(mi, 32) + span(mf, 64))
    for start in (mx, mv, mo):
        for c in range(4):
            pick(span(start + c * P))
    both = np.concatenate([a["w_proj_a_2"][0], a["w_proj_b_2"][0]], axis=0)
    for m in range(DC):
        pick(span(ga + m * P))
        pick(span(gb + m * P))
        take(both, m)
    for m in range(DC):
        take(a["w_out_2"][0], m)
    mlp([a["ffn2_w_gate_2"][0], a["ffn2_w_up_2"][0]], a["ffn2_w_down_2"][0], FFN_GROUPS)
    assert len(blocks) == N_BLOCKS
    return np.ascontiguousarray(np.stack(blocks).transpose(0, 2, 1, 3).reshape(N_BLOCKS, P, KC * P))


def small_params(a):
    out = np.zeros((P, n_param), np.float32)

    def put(name, value):
        c, n = PARAMS[name]
        out[:value.shape[0], c:c + n] = value

    for name, gain in (("g_mix0", a["g_mix"][0]), ("g_mix1", a["g_mix"][1]), ("g_mlp0", a["g_mlp"][0]),
                       ("g_mlp1", a["g_mlp"][1]), ("g_final", a["g_final"]), ("ffn1_norm", a["ffn1_norm_2"][0]),
                       ("mix_norm", a["mix_norm_2"][0]), ("ffn2_norm", a["ffn2_norm_2"][0])):
        put(name, gain.reshape(DC, P).T)
    for name in ("q_norm", "k_norm", "idx_k_norm"):
        put(name, np.concatenate([a[name + "_2"][0]] * 2)[:, None])
    put("conv_w", a["conv_w_2"][0].reshape(CONV, 4, P).transpose(2, 1, 0).reshape(P, 4 * CONV))
    put("conv_b", a["conv_b_2"][0].reshape(4, P).T)
    put("b_i", a["b_i_2"][0][:, None])
    put("b_f", a["b_f_2"][0][:, None])
    put("head_norm", a["m_head_norm_2"][0].reshape(ML_HEADS, P).T)
    put("w_mqk", np.stack([a["w_mq_2"][0], a["w_mk_2"][0]], axis=1).transpose(2, 0, 1, 3).reshape(P, -1))
    return out


def shape_tables():
    i = np.arange(P)
    common = np.zeros((P, 4, P), np.float32)
    common[:, 0] = np.eye(P)
    common[:, 1] = -(i[:, None] >= i[None, :]).astype(np.float32)
    common[:, 2] = -BIG * (i[:, None] >= i[None, :])
    common[:, 3] = (i[:, None] // ATT_DIM == i[None, :] // ATT_DIM) / ATT_DIM
    ret = np.zeros((P, 2 + RET_HEADS, T), np.float32)
    half = RET_QK // 2
    inv_freq = (1.0 / (10000.0 ** np.linspace(0.0, 1.0, half, dtype=np.float32))).astype(np.float32)
    angle = inv_freq[:, None] * np.arange(T, dtype=np.float32)[None, :]
    ret[:, 0], ret[:, 1] = np.cos(angle), np.sin(angle)
    rel = (np.arange(T)[None, :] - i[:, None]).astype(np.float64)
    for hd in range(RET_HEADS):
        log_gamma = float(np.log1p(-np.exp2(np.float32(-5.0 - hd))))
        ret[:, 2 + hd] = np.where(rel >= 0, np.exp(log_gamma * np.maximum(rel, 0)), 0)
    mix = np.zeros((P, 6, P), np.float32)
    for hd in range(ML_HEADS):
        mix[hd, hd] = 1.0
    mix[:, 4] = BIG * (i[:, None] > i[None, :])
    mix[:, 5] = 1.0 / ML_V
    return common, ret, mix


def kernel(**inputs):
    import concourse.bacc as bacc
    from concourse.bass_utils import run_bass_kernel_spmd

    a = {name: np.asarray(value) for name, value in inputs.items()}
    common, ret, mix = shape_tables()
    arrays = {"in_stream": weight_stream(a), "in_params": small_params(a), "in_tables": common,
              "in_tables_ret": ret, "in_tables_mix": mix, "in_x": np.ascontiguousarray(a["x"][0])}
    nc = bacc.Bacc("TRN2", target_bir_lowering=False, num_devices=1)
    aps = [nc.dram_tensor(name, value.shape, F32, kind="ExternalInput").ap() for name, value in arrays.items()]
    out = nc.dram_tensor("out_x", (T, D), F32, kind="ExternalOutput").ap()
    build(nc, *aps, out)
    result = run_bass_kernel_spmd(nc, [arrays], core_ids=[0])
    return result.results[0]["out_x"].reshape(1, T, D)
```

```python
from contextlib import ExitStack

import numpy as np

import concourse.bass as bass
from concourse import mybir

F32 = mybir.dt.float32
F32R = mybir.dt.float32r
ALU = mybir.AluOpType
ACT = mybir.ActivationFunctionType
AX_X = mybir.AxisListType.X

SBUF_BYTES = 224 * 1024 - 32
P = 128
T = 512
TB = T // P
D = 1024
DC = D // P
KC = 8
EPS = 1e-6
BIG = 1e30
OUT_OF_REACH = -1e38
TAKEN = -3e38
HIDDEN = 4096
MLP_GROUPS = (KC,) * (HIDDEN // (KC * P))
SB_HEADS, SB_DIM = 16, 64
RET_HEADS, RET_QK, RET_V = 4, 256, 512
D_FF = 2816
FFN_GROUPS = (8, 8, 6)
ATT_HEADS, ATT_KV, ATT_DIM = 8, 2, 64
IDX_HEADS, IDX_DIM = 8, 64
TOPK, CHUNK = 128, 64
ML_HEADS, ML_QK, ML_V, CONV = 4, 64, 128, 4
assert sum(FFN_GROUPS) * P == D_FF and TOPK == min(256, T // 4) and TOPK % 8 == 0

PARAMS, n_param = {}, 0
for _name, _count in (("g_mix0", DC), ("g_mlp0", DC), ("g_mix1", DC), ("g_mlp1", DC), ("g_final", DC),
                      ("ffn1_norm", DC), ("mix_norm", DC), ("ffn2_norm", DC), ("q_norm", 1), ("k_norm", 1),
                      ("idx_k_norm", 1), ("conv_w", 4 * CONV), ("conv_b", 4), ("b_i", 1), ("b_f", 1),
                      ("head_norm", ML_HEADS), ("w_mqk", ML_HEADS * 2 * ML_QK)):
    PARAMS[_name] = (n_param, _count)
    n_param += _count

MIX_K, MIX_Q, MIX_V, MIX_IK, MIX_IQ, MIX_GATES, MIX_MX, MIX_MV, MIX_MO, MIX_BLOCKS = 0, 2, 6, 7, 8, 12, 13, 17, 21, 25
GATE_IW, GATE_I, GATE_F = 0, 32, 64

RET_QKV, RET_G = 8, 4
RUN_AT, N_BLOCKS = {}, 0
for _name, _count in (("sb", 3 * DC), ("sb_out", DC), ("mlp0", 2 * DC * len(MLP_GROUPS)),
                      ("ret", RET_HEADS * (RET_QKV + RET_G)), ("ret_out", 2 * DC),
                      ("mlp1", 2 * DC * len(MLP_GROUPS)), ("ffn1", 2 * D_FF // P + DC * len(FFN_GROUPS)),
                      ("mix", MIX_BLOCKS - MIX_GATES), ("mix_late", MIX_GATES), ("gates", 2 * DC),
                      ("proj", DC), ("w_out", DC),
                      ("ffn2", 2 * D_FF // P + DC * len(FFN_GROUPS))):
    RUN_AT[_name] = N_BLOCKS
    N_BLOCKS += _count

LATE_PER_HEAD = MIX_GATES // ML_HEADS
GATES_PER_SELECTION, GATE_STEPS = 4, (3, 11, 19, 27)
assert GATES_PER_SELECTION * (TB - 1) + len(GATE_STEPS) == 2 * DC


def gate_chunk(i):
    early = GATES_PER_SELECTION * (TB - 1)
    return MIX_MX + i if i < early else MIX_IQ + i - early


def mix_block(m):
    return RUN_AT["mix"] + m - MIX_GATES if m >= MIX_GATES else RUN_AT["mix_late"] + m


HEAD_NORMED = {MIX_K: "k_norm", MIX_K + 1: "k_norm", MIX_IK: "idx_k_norm"} | {MIX_Q + c: "q_norm" for c in range(4)}

NEG_AT = [0, P, 3 * P, 6 * P]

NORMS = [("g_mix0", None), ("g_mlp0", RUN_AT["sb_out"]), ("g_mix1", RUN_AT["ret"] - DC),
         ("g_mlp1", RUN_AT["mlp1"] - DC), ("g_final", RUN_AT["ffn1"] - DC), ("ffn1_norm", None),
         ("mix_norm", RUN_AT["mix"] - DC), ("ffn2_norm", RUN_AT["w_out"])]
N_MIX0, N_MLP0, N_MIX1, N_MLP1, N_FINAL, N_FFN1, N_MIX, N_FFN2 = range(8)

Z_AT = {(0, 0): 0, (0, 1): 512, (0, 3): 896, (0, 2): 1024, (1, 2): 1280, (1, 0): 1536, (1, 1): 2048, (1, 3): 2432}
Z_BANKS = 5
S_AT = {0: 0, 1: 512, 3: 896, 2: 1024}


def seen_by(kb):
    return T - kb * P


def place_of(n):
    return n if isinstance(n, tuple) else (n, None)


def number(n, plus=0):
    c, r = place_of(n)
    return c + plus if r is None else r * 2 + (c + plus)


def later(n, k):
    c, r = place_of(n)
    return (c + k, r)


def slot(n):
    return place_of(n)[0] % 2


def turn(n, plus=0):
    c, r = place_of(n)
    return c // 2 + plus if r is None else r + (c // 2 + plus)


def pairs(eng, first, blocks, body, step=2, peel=False):
    turns = blocks // step
    assert turns * step == blocks and step % 2 == 0
    if turns == 1 or peel:
        body((first, None), None)
    if turns == 1:
        return
    with eng.Fori(int(peel), turns) as t:
        body((first, t * (step // 2)), t)


def at(t, scale, plus):
    return bass.ds(plus if t is None else t * scale + plus, 1)


def flat(ap):
    return ap.rearrange("p a b -> p (a b)")


def build(nc, stream, params, tables, tables_ret, tables_mix, x_in, out):
    with ExitStack() as ctx:
        where = [(nc.sbuf_base + 63) // 64 * 64]

        def sb(name, shape, dt=F32, over=None):
            size = int(np.prod(shape[1:])) * 4
            spot = where[0] if over is None else over
            t = nc.alloc_sbuf_tensor_at(name, shape, dt, offset=spot)
            if over is None:
                where[0] += (size + 31) // 32 * 32
            return t

        def sem(name):
            return ctx.enter_context(nc.semaphore(name))

        h = sb("h", [P, DC, T])
        x_hi = sb("x_hi", [P, DC, T], F32R)
        x_lo = sb("x_lo", [P, DC, T], F32R)
        raw = sb("raw", [P, 2, KC, P])
        w_hi = sb("w_hi", [P, 2, KC, P], F32R)
        w_lo = sb("w_lo", [P, 2, KC, P], F32R)
        prm = sb("prm", [P, n_param])
        tab = sb("tab", [P, 4, P])
        ident, neg_tri, strict, head_mean = (tab[:, i] for i in range(4))
        ones = sb("ones", [P, 4, P])
        mean_d, mean_v, one, neg_one = (ones[:, i] for i in range(4))
        eps = sb("eps", [P, 1])
        std = sb("std", [P, T])
        rstd = sb("rstd", [P, T], over=SBUF_BYTES - T * 4)
        u_sum = rstd
        sq_sum = rstd
        inv = sb("inv", [P, T])
        xn = sb("xn", [P, 2, T])
        arena = where[0]

        def col(name, i=0, rows=P):
            c = PARAMS[name][0] + i
            return prm[0:rows, c:c + 1]

        where[0] = arena
        u_hi = sb("u_hi", [P, 2, KC, T], F32R)
        u_lo = sb("u_lo", [P, 2, KC, T], F32R)
        u_act = sb("u_act", [P, T])
        u = sb("u", [P, 2, T])
        where[0] = arena
        x_tok = sb("x_tok", [P, TB, D])
        where[0] = arena
        o_hi = sb("o_hi", [P, DC, T], F32R)
        o_lo = sb("o_lo", [P, DC, T], F32R)
        sb_q = sb("sb_q", [P, T])
        sb_k = sb("sb_k", [P, T])
        sb_v = sb("sb_v", [P, T])
        sb_vt = sb("sb_vt", [P, TB, P])
        z_sp = sb("z_sp", [P, Z_BANKS, T])
        z_ex = sb("z_ex", [P, Z_BANKS, T])
        where[0] = arena
        y_hi = sb("y_hi", [P, 2 * DC, T], F32R)
        y_lo = sb("y_lo", [P, 2 * DC, T], F32R)
        tab_ret = sb("tab_ret", [P, 2 + RET_HEADS, T])
        r_q = sb("r_q", [P, 2, T])
        r_k = sb("r_k", [P, 2, T])
        r_x = sb("r_x", [P, 2, T])
        r_t = sb("r_t", [P, 2, T])
        r_v = sb("r_v", [P, TB, RET_V])
        r_g = sb("r_g", [P, 4, T])
        r_p = sb("r_p", [P, 1280])
        r_o = sb("r_o", [P, 4, T])
        r_sq = [xn[:, 0], xn[:, 1], r_x[:, 0], r_x[:, 1]]
        where[0] = arena
        pj_at = where[0]
        pj = sb("pj", [P, MIX_BLOCKS, T])
        ya_hi = sb("ya_hi", [P, 4, T], F32R)
        ya_lo = sb("ya_lo", [P, 4, T], F32R)
        yb_hi = sb("yb_hi", [P, 4, T], F32R)
        yb_lo = sb("yb_lo", [P, 4, T], F32R)
        tab_mix = sb("tab_mix", [P, 6, P])
        later_keys, mean_h = tab_mix[:, 4], tab_mix[:, 5]
        a_v = sb("a_v", [P, TB, P])
        m_v_at = where[0]
        m_v = sb("m_v", [P, TB, 4 * P])
        iw = sb("iw", [P, TB, IDX_HEADS])
        scratch = where[0]
        n_sq = sb("n_sq", [P, 2, T])
        n_std = sb("n_std", [P, 2, T])
        n_r = sb("n_r", [P, 2, T])
        m_xc = sb("m_xc", [P, 4, T], over=pj_at + MIX_MV * T * 4)
        where[0] = pj_at + MIX_MX * T * 4
        m_q = sb("m_q", [ML_QK, T])
        m_k = sb("m_k", [ML_QK, T])
        m_h = sb("m_h", [P, T])
        m_so = sb("m_so", [P, T])
        where[0] = scratch
        g_li = sb("g_li", [ML_HEADS, T])
        g_lf = sb("g_lf", [ML_HEADS, T])
        g_sum = sb("g_sum", [ML_HEADS, T])
        g_a = sb("g_a", [ML_HEADS, T])
        g_max = sb("g_max", [ML_HEADS, T])
        m_a = sb("m_a", [P, TB, ML_HEADS])
        m_w = sb("m_w", [P, 1280])
        where[0] = scratch
        score = sb("score", [P, T])
        neg = sb("neg", [P, 1280])
        rr = sb("rr", [P, 2, T])
        s_m = sb("s_m", [P, 2, T])
        stat = sb("stat", [P, 4, ATT_HEADS * TB])
        best = sb("best", [P, 8])
        assert where[0] <= SBUF_BYTES - T * 4
        where[0] = arena
        mg_hi = sb("mg_hi", [P, DC, T], F32R)
        mg_lo = sb("mg_lo", [P, DC, T], F32R, over=m_v_at)
        assert MIX_IQ >= DC and m_v_at + DC * T * 4 <= SBUF_BYTES - T * 4

        ps = ctx.enter_context(nc.psum_tensor("ps", [P, 8, T], F32))
        GEMM_BANK = 6

        raw_full = [sem("raw_full_0"), sem("raw_full_1")]
        hi_done = sem("hi_done")
        lo_done = sem("lo_done")
        mm_done = sem("mm_done")
        bank_free = [sem("bank_free_0"), sem("bank_free_1")]
        made = {}

        def sig(name):
            if name not in made:
                made[name] = sem(name)
            return made[name]

        block = ctx.enter_context(nc.Block())

        @block.sync
        def _(sp):
            sp.dma_start(x_tok[:], x_in.rearrange("(b p) d -> p b d", p=P)).then_inc(sig("x_in"), 16)
            sp.dma_start(tab[:], tables).then_inc(sig("tables_in"), 16)
            sp.dma_start(prm[:], params).then_inc(sig("tables_in"), 16)

            def load(n):
                sp.wait_ge(lo_done, number(n, 1))
                sp.dma_start(raw[:, slot(n)], stream[bass.ds(number(n), 1)].rearrange(
                    "a p (k m) -> p (a k) m", m=P)).then_inc(raw_full[slot(n)], 16)

            def load_two(n, _):
                load(n)
                load(later(n, 1))

            def load_run(first, last):
                if first % 2:
                    load(first)
                    first += 1
                pairs(sp, first, (last - first) // 2 * 2, load_two)
                if (last - first) % 2:
                    load(last - 1)

            load_run(0, RUN_AT["ret"] - DC)
            sp.wait_ge(sig("ul_done"), HIDDEN // P)
            sp.dma_start(tab_ret[:], tables_ret).then_inc(sig("tables_ret_in"), 16)
            load_run(RUN_AT["ret"] - DC, RUN_AT["mlp1"] + DC)
            sp.wait_ge(mm_done, RUN_AT["mlp1"] + 2 + 1)
            sp.dma_start(tab_mix[:], tables_mix).then_inc(sig("tables_mix_in"), 16)
            load_run(RUN_AT["mlp1"] + DC, N_BLOCKS)
            sp.wait_ge(sig("out_ready"), 2 * TB)
            sp.dma_start(out.rearrange("(b p) d -> p b d", p=P), x_tok[:]).then_inc(sig("stored"), 16)
            sp.wait_ge(sig("stored"), 16)

        @block.scalar
        def _(act):
            def split_hi(n):
                if place_of(n)[1] is None and number(n) >= N_BLOCKS:
                    return
                act.wait_ge(raw_full[slot(n)], turn(n, 1) * 16)
                act.wait_ge(mm_done, number(n, 1))
                nc.scalar.activation(w_hi[:, slot(n)], raw[:, slot(n)], ACT.Copy).then_inc(hi_done, 1)

            def product(n):
                act.wait_ge(mm_done, number(n, 3))
                return ps[:, GEMM_BANK + slot(n)]

            def freed(n):
                act.wait_ge(bank_free[slot(n)], turn(n, 2))

            def chunk(k, c):
                name, first = NORMS[k]
                if first is not None:
                    freed(first + c)
                elif k == N_MIX0:
                    act.wait_ge(sig("h_in"), c + 1)
                else:
                    act.wait_ge(sig("final_done"), c + 1)
                if k != N_FINAL:
                    nc.scalar.activation(x_hi[:, c], h[:, c], ACT.Copy, scale=col(name, c)).then_inc(sig("xh_done"), 1)
                if c >= 2:
                    act.wait_ge(sig("sum_done"), k * DC + c - 1)
                nc.scalar.activation(xn[:, c % 2], h[:, c], ACT.Square).then_inc(sig("sq_done"), 1)

            def root(k):
                act.wait_ge(sig("ms_done"), k + 1)
                nc.scalar.activation(std[:], ps[:, 5], ACT.Sqrt, bias=eps[:]).then_inc(sig("std_done"), 1)

            act.wait_ge(sig("consts"), 5)
            act.wait_ge(sig("tables_in"), 32)
            split_hi(0)
            for c in range(DC):
                chunk(N_MIX0, c)

            split_hi(1)
            root(N_MIX0)
            split_hi(2)
            split_hi(3)

            def sb_pair(n, t, pc, step, dense=True):
                p = pc if t is None else t * step + pc
                if dense:
                    split_hi(later(n, 1))
                for z in range(Z_BANKS):
                    act.wait_ge(sig("abs_done"), p * Z_BANKS + (z + 1))
                    nc.scalar.activation(z_ex[:, z], z_ex[:, z], ACT.Exp, scale=-1.0).then_inc(sig("exp_done"), 1)
                if dense:
                    split_hi(later(n, 2))
                for z in range(Z_BANKS):
                    act.wait_ge(sig("exp_done"), p * Z_BANKS + (z + 1))
                    nc.scalar.activation(z_ex[:, z], z_ex[:, z], ACT.Ln, bias=1.0).then_inc(sig("ln_done"), 1)
                act.wait_ge(sig("cum_done"), p + 1)
                for z in range(Z_BANKS):
                    act.wait_ge(sig("sp_done"), p * Z_BANKS + (z + 1))
                    nc.scalar.activation(z_ex[:, z], ps[:, z], ACT.Exp).then_inc(sig("a_done"), 1)
                if dense:
                    split_hi(later(n, 3))
                act.wait_ge(sig("av_done"), p + 1)
                nc.scalar.activation(flat(o_hi[:, at(t, step, pc)]), ps[:, 5], ACT.Copy).then_inc(sig("oh_done"), 1)

            def sb_two(n, t):
                sb_pair(n, t, 0, 2)
                sb_pair(later(n, 3), t, 1, 2)

            pairs(act, 3, 6 * 3, sb_two, step=6)
            sb_pair(3 * 7, None, 6, 0)
            sb_pair(None, None, 7, 0, dense=False)

            def ahead(first, blocks):
                def two(n, _):
                    split_hi(later(n, 1))
                    split_hi(later(n, 2))
                if first + blocks == N_BLOCKS:
                    pairs(act, first, blocks - 2, two)
                    two(N_BLOCKS - 2, None)
                else:
                    pairs(act, first, blocks, two)

            def ahead_of_norm(first, k):
                for c in range(DC):
                    split_hi(first + c + 1)
                    if c >= 1:
                        chunk(k, c - 1)
                chunk(k, DC - 1)

            ahead_of_norm(RUN_AT["sb_out"], N_MLP0)

            def hidden_hi(t, scale, plus, done, group):
                act.wait_ge(sig("u_done"), done)
                nc.scalar.activation(flat(u_hi[:, group % 2, at(t, scale, plus)]), u[:, plus],
                                     ACT.Copy).then_inc(sig("uh_done"), 1)

            def mlp(first, chunks_before, norm, next_norm):
                def up(n, t, group, before):
                    for i in range(2):
                        split_hi(later(n, i + 1))
                        if t is None and i == 0 and group == 0:
                            root(norm)
                        done = before + i + 1 if t is None else t * 2 + (before + i + 1)
                        m = later(n, i)
                        freed(m)
                        nc.scalar.activation(u[:, i], u_act[:], ACT.Square).then_inc(sig("u_done"), 1)
                        hidden_hi(t, 2, i, done, group)
                groups(MLP_GROUPS, first, chunks_before, 1, up, next_norm)

            def ffn(first, chunks_before, norm, next_norm):
                def up(n, t, group, before):
                    split_hi(later(n, 1))
                    if t is None and group == 0:
                        root(norm)
                    freed(n)
                    nc.scalar.activation(u_act[:], u_act[:], ACT.Silu).then_inc(sig("silu_done"), 1)
                    split_hi(later(n, 2))
                    hidden_hi(t, 1, 0, before + 1 if t is None else t + (before + 1), group)
                groups(FFN_GROUPS, first, chunks_before, 2, up, next_norm)

            def groups(sizes, first, chunks_before, per_chunk, up, next_norm):
                n = first
                for g in range(len(sizes) + 1):
                    if g < len(sizes):
                        before = chunks_before + sum(sizes[:g])
                        pairs(act, n, sizes[g] * per_chunk, lambda m, t: up(m, t, g, before), peel=(g == 0))
                        n += sizes[g] * per_chunk
                    if g == len(sizes) and next_norm is not None:
                        ahead_of_norm(n, next_norm)
                    elif g >= 1:
                        ahead(n, DC)
                        n += DC

            mlp(RUN_AT["mlp0"], 0, N_MLP0, N_MIX1)

            def count(t, scale, plus):
                return plus if t is None else t * scale + plus

            def r_head(n, t, i, dense=True):
                if dense:
                    for j in range(4):
                        split_hi(later(n, j + 1))
                for e in range(4):
                    act.wait_ge(sig("rav_done"), count(t, 4, 4 * i + e + 1))
                    nc.scalar.activation(r_o[:, e], ps[:, e], ACT.Copy).then_inc(sig("ro_done"), 1)
                if dense:
                    for j in range(4):
                        split_hi(later(n, 4 + j + 1))
                for e in range(4):
                    act.wait_ge(sig("cen_done"), count(t, 4, 4 * i + e + 1))
                    nc.scalar.activation(r_sq[e], r_o[:, e], ACT.Square).then_inc(sig("rsq_done"), 1)
                gate = later(n, RET_QKV if dense else 0)
                for e in range(4):
                    if e == 2:
                        act.wait_ge(sig("rvar_done"), count(t, 4, 4 * i + 4))
                        nc.scalar.activation(std[:], ps[:, 5], ACT.Sqrt, bias=eps[:]).then_inc(sig("rstd_in"), 1)
                    split_hi(later(gate, e + 1))
                    freed(later(gate, e))
                    nc.scalar.activation(r_g[:, e], r_g[:, e], ACT.Silu).then_inc(sig("rgate_done"), 1)
                for e in range(4):
                    act.wait_ge(sig("ry_done"), count(t, 4, 4 * i + e + 1))
                    nc.scalar.activation(flat(y_hi[:, at(t, 4, 4 * i + e)]), r_o[:, e],
                                         ACT.Copy).then_inc(sig("yh_done"), 1)

            for j in range(RET_QKV):
                split_hi(RUN_AT["ret"] + j + 1)
                if j == 0:
                    root(N_MIX1)
            pairs(act, RUN_AT["ret"] + RET_QKV, 12 * (RET_HEADS - 1), lambda n, t: r_head(n, t, 0), step=12)
            r_head(RUN_AT["ret_out"] - RET_G, None, RET_HEADS - 1, dense=False)
            ahead(RUN_AT["ret_out"], DC)
            ahead_of_norm(RUN_AT["ret_out"] + DC, N_MLP1)
            mlp(RUN_AT["mlp1"], HIDDEN // P, N_MLP1, N_FINAL)
            root(N_FINAL)
            for c in range(DC):
                chunk(N_FFN1, c)
            ffn(RUN_AT["ffn1"], 2 * HIDDEN // P, N_FFN1, N_MIX)

            split_hi(RUN_AT["mix"] + 1)
            root(N_MIX)
            split_hi(RUN_AT["mix"] + 2)
            ahead(RUN_AT["mix"] + 2, MIX_BLOCKS - MIX_GATES - 3)
            split_hi(RUN_AT["mix_late"])

            for c in range(4):
                act.wait_ge(sig("vt_mix"), 1 + c)
                nc.scalar.activation(m_v[:, :, c * P:(c + 1) * P],
                                     ps[:, 1 + c].rearrange("p (b f) -> p b f", b=TB), ACT.Copy).then_inc(sig("vt_moved"), 1)

            for c in range(4):
                act.wait_ge(sig("conv_done"), c + 1)
                nc.scalar.activation(m_xc[:, c], m_xc[:, c], ACT.Silu).then_inc(sig("xc_done"), 1)
            gate = pj[:, MIX_GATES]
            nc.scalar.activation(g_li[:], gate[GATE_I:GATE_I + ML_HEADS], ACT.Identity,
                                 bias=col("b_i", rows=ML_HEADS)).then_inc(sig("gate_done"), 1)
            nc.scalar.activation(g_lf[:], gate[GATE_F:GATE_F + ML_HEADS], ACT.Identity,
                                 bias=col("b_f", rows=ML_HEADS)).then_inc(sig("gate_done"), 1)
            act.wait_ge(sig("gabs_done"), 1)
            nc.scalar.activation(g_sum[:], g_sum[:], ACT.Exp, scale=-1.0).then_inc(sig("gexp_done"), 1)
            act.wait_ge(sig("gexp_done"), 1)
            nc.scalar.activation(g_sum[:], g_sum[:], ACT.Ln, bias=1.0).then_inc(sig("gexp_done"), 1)
            act.wait_ge(sig("ma_in"), 1)
            nc.scalar.activation(m_a[:], ps[:, 0, 0:TB * ML_HEADS].rearrange("p (b f) -> p b f", b=TB),
                                 ACT.Copy).then_inc(sig("ma_done"), 1)
            act.wait_ge(sig("ma_done"), 1)
            for hd in range(ML_HEADS):
                late = RUN_AT["mix_late"] + LATE_PER_HEAD * hd
                act.wait_ge(sig("mqk_done"), hd + 1)
                nc.scalar.activation(m_q[:], ps[0:ML_QK, 1], ACT.Copy, scale=ML_QK ** -0.5).then_inc(sig("mq_moved"), 1)
                nc.scalar.activation(m_k[:], ps[0:ML_QK, 2], ACT.Copy).then_inc(sig("mq_moved"), 1)
                split_hi(late + 1)
                act.wait_ge(sig("mmax_done"), hd + 1)
                for kb in range(TB):
                    nc.scalar.activation(m_w[:, S_AT[kb]:S_AT[kb] + P], ps[:, 4, kb * P:(kb + 1) * P], ACT.Exp,
                                         scale=-1.0, bias=m_a[:, kb, hd:hd + 1]).then_inc(sig("mexp_done"), 1)
                for kb in range(TB - 1):
                    nc.scalar.activation(m_w[:, S_AT[kb] + P:S_AT[kb] + seen_by(kb)], ps[:, 3, (kb + 1) * P:T],
                                         ACT.Exp, scale=-1.0, bias=m_a[:, kb, hd:hd + 1]).then_inc(sig("mexp_done"), 1)
                nc.scalar.activation(xn[:, 0], ps[:, 5], ACT.Exp, scale=-1.0).then_inc(sig("mexp_done"), 1)
                nc.scalar.activation(m_so[:], pj[:, MIX_MO + hd], ACT.Sigmoid).then_inc(sig("mso_done"), 1)
                split_hi(late + 2)
                act.wait_ge(sig("mh_done"), 3 * hd + 1)
                nc.scalar.activation(xn[:, 1], m_h[:], ACT.Square).then_inc(sig("msq_done"), 1)
                split_hi(late + 3)
                act.wait_ge(sig("mvar_done"), hd + 1)
                nc.scalar.activation(std[:], ps[:, 0], ACT.Sqrt, bias=eps[:]).then_inc(sig("mstd_done"), 1)
                act.wait_ge(sig("mh_done"), 3 * hd + 3)
                nc.scalar.activation(yb_hi[:, hd], m_h[:], ACT.Copy).then_inc(sig("yb_hi_done"), 1)

            act.wait_ge(sig("yb_lo_done"), ML_HEADS)
            act.wait_ge(sig("vt_mix"), 6)
            nc.scalar.activation(a_v[:].rearrange("p b f -> p (b f)"), ps[:, 0], ACT.Copy).then_inc(sig("vt_moved"), 1)

            for j, m in enumerate(HEAD_NORMED):
                if j >= 2:
                    act.wait_ge(sig("hms_done"), j - 1)
                nc.scalar.activation(n_sq[:, j % 2], pj[:, m], ACT.Square).then_inc(sig("hsq_done"), 1)
                act.wait_ge(sig("hms_done"), j + 1)
                if j >= 2:
                    act.wait_ge(sig("hr_done"), j - 1)
                nc.scalar.activation(n_std[:, j % 2], ps[:, j % 2], ACT.Sqrt, bias=eps[:]).then_inc(sig("hstd_done"), 1)

            for j in range(3 * IDX_HEADS):
                seen = (1 + j // IDX_HEADS + 1) * P
                act.wait_ge(sig("ilog_done"), j + 1)
                if j >= 2:
                    act.wait_ge(sig("iacc_done"), j - 1)
                nc.scalar.activation(rr[:, j % 2, 0:seen], ps[:, j % 2, 0:seen], ACT.Relu).then_inc(sig("irelu_done"), 1)
                if j % IDX_HEADS == IDX_HEADS - 1:
                    for i in range(GATES_PER_SELECTION):
                        split_hi(RUN_AT["gates"] + j // IDX_HEADS * GATES_PER_SELECTION + i + 1)
            def att_weights(j):
                tb = j // 2 % TB
                seen = (tb + 1) * P
                act.wait_ge(sig("amax_done"), j + 1)
                nc.scalar.activation(s_m[:, j % 2, 0:seen], s_m[:, j % 2, 0:seen], ACT.Exp, scale=ATT_DIM ** -0.5,
                                     bias=stat[:, 1, j:j + 1], accum_out=stat[:, 2, j:j + 1]).then_inc(sig("aexp_done"), 1)

            def att_turned(j):
                tb = j // 2 % TB
                seen = (tb + 1) * P
                act.wait_ge(sig("aturn_done"), j + 1)
                if j >= 2:
                    act.wait_ge(sig("apv_done"), j - 1)
                nc.scalar.activation(rr[:, j % 2, 0:seen], ps[:, 2 + j % 2, 0:seen], ACT.Copy).then_inc(sig("pt_done"), 1)

            n_att = ATT_HEADS * TB
            for j in range(n_att + 1):
                if j in GATE_STEPS:
                    split_hi(RUN_AT["proj"] - len(GATE_STEPS) + GATE_STEPS.index(j) + 1)
                if j < n_att:
                    att_weights(j)
                if j >= 1:
                    att_turned(j - 1)
                    if (j - 1) % 8 == 7:
                        c = (j - 1) // 8
                        act.wait_ge(sig("apv_done"), j)
                        nc.scalar.activation(ya_hi[:, c], ps[:, 4 + c % 2], ACT.Copy).then_inc(sig("ya_hi_done"), 1)

            for m in range(DC):
                split_hi(RUN_AT["proj"] + m + 1)
                for i in range(2):
                    if m == 0:
                        freed(RUN_AT["proj"] - 2 + i)
                    nc.scalar.activation(xn[:, i], pj[:, gate_chunk(2 * m + i)], ACT.Sigmoid).then_inc(sig("mgate_done"), 1)
                act.wait_ge(sig("mg_done"), m + 1)
                nc.scalar.activation(mg_hi[:, m], u_sum[:], ACT.Copy).then_inc(sig("mg_hi_done"), 1)
            ahead_of_norm(RUN_AT["w_out"], N_FFN2)
            ffn(RUN_AT["ffn2"], 2 * HIDDEN // P + D_FF // P, N_FFN2, None)
            for i in range(2 * TB):
                act.wait_ge(sig("out_turned"), i + 1)
                nc.scalar.activation(x_tok[:, i // 2, (i % 2) * T:(i % 2 + 1) * T], ps[:, i % 4], ACT.Copy).then_inc(
                    sig("out_ready"), 1)

        @block.vector
        def _(dve):
            dve.sem_inc(lo_done, 2)
            dve.sem_inc(bank_free[0], 1)
            dve.sem_inc(bank_free[1], 1)

            def split_lo(n):
                if place_of(n)[1] is None and number(n) >= N_BLOCKS:
                    return
                dve.wait_ge(hi_done, number(n, 1))
                nc.vector.tensor_tensor(w_lo[:, slot(n)], raw[:, slot(n)], w_hi[:, slot(n)].bitcast(F32),
                                        ALU.subtract).then_inc(lo_done, 1)

            def product(n):
                dve.wait_ge(mm_done, number(n, 3))
                return ps[:, GEMM_BANK + slot(n)]

            def count(t, scale, plus):
                return plus if t is None else t * scale + plus

            def scaled(n, dst, scale=1.0, op=ALU.mult):
                nc.vector.scalar_tensor_tensor(out=dst, in0=product(n), scalar=scale, in1=inv[:], op0=op,
                                               op1=ALU.mult).then_inc(bank_free[slot(n)], 1)

            split_norms = [k for k in range(len(NORMS)) if k != N_FINAL]

            def low(k, c):
                dve.wait_ge(sig("xh_done"), split_norms.index(k) * DC + c + 1)
                nc.vector.scalar_tensor_tensor(out=x_lo[:, c], in0=h[:, c], scalar=col(NORMS[k][0], c),
                                               in1=x_hi[:, c].bitcast(F32), op0=ALU.mult,
                                               op1=ALU.subtract).then_inc(sig("xl_done"), 1)

            def inverse(k):
                dve.wait_ge(sig("std_done"), k + 1)
                nc.vector.reciprocal(inv[:], std[:]).then_inc(sig("inv_done"), 1)
                dve.wait_ge(sig("inv_done"), k + 1)

            for c in range(DC):
                dve.wait_ge(sig("x_turned"), c + 1)
                nc.vector.tensor_copy(h[:, c], ps[:, c % 4]).then_inc(sig("h_in"), 1)
            dve.wait_ge(sig("h_in"), DC)
            dve.wait_ge(sig("tables_in"), 32)
            split_lo(0)
            for c in range(DC):
                low(N_MIX0, c)

            def sb_values(p):
                dve.wait_ge(sig("sbvt_done"), p)
                nc.vector.tensor_copy(sb_vt[:].rearrange("p b f -> p (b f)"), ps[:, 4]).then_inc(sig("sbv_done"), 1)

            pair_of = (sb_q, sb_k, sb_v)
            for which in range(3):
                split_lo(which + 1)
                if which == 0:
                    inverse(N_MIX0)
                scaled(which, pair_of[which][:], 1.0 if which else SB_DIM ** -0.5)
            sb_values(1)

            def sb_pair(n, t, pc, step, dense=True):
                p = pc if t is None else t * step + pc
                if dense:
                    split_lo(later(n, 1))
                for z in range(Z_BANKS):
                    dve.wait_ge(sig("z_done"), p + 1)
                    nc.vector.tensor_copy(z_sp[:, z], ps[:, z]).then_inc(sig("zc_done"), 1)
                    dve.wait_ge(sig("zc_done"), p * Z_BANKS + (z + 1))
                    nc.vector.scalar_tensor_tensor(out=z_ex[:, z], in0=z_sp[:, z], scalar=-1.0, in1=z_sp[:, z],
                                                   op0=ALU.mult, op1=ALU.max).then_inc(sig("abs_done"), 1)
                if dense:
                    scaled(n, sb_q[:], SB_DIM ** -0.5)
                    split_lo(later(n, 2))
                for z in range(Z_BANKS):
                    dve.wait_ge(sig("ln_done"), p * Z_BANKS + (z + 1))
                    nc.vector.scalar_tensor_tensor(out=z_sp[:, z], in0=z_sp[:, z], scalar=0.0, in1=z_ex[:, z],
                                                   op0=ALU.max, op1=ALU.add).then_inc(sig("sp_done"), 1)
                if dense:
                    scaled(later(n, 1), sb_k[:])
                    split_lo(later(n, 3))
                    scaled(later(n, 2), sb_v[:])
                dve.wait_ge(sig("oh_done"), p + 1)
                nc.vector.tensor_tensor(flat(o_lo[:, at(t, step, pc)]), ps[:, 5],
                                        flat(o_hi[:, at(t, step, pc)]).bitcast(F32), ALU.subtract).then_inc(sig("ol_done"), 1)
                if dense:
                    sb_values(p + 2)

            def sb_two(n, t):
                sb_pair(n, t, 0, 2)
                sb_pair(later(n, 3), t, 1, 2)

            pairs(dve, 3, 6 * 3, sb_two, step=6)
            sb_pair(3 * 7, None, 6, 0)
            sb_pair(None, None, 7, 0, dense=False)

            def residual(first, blocks, scale=1.0):
                def two(n, t):
                    for i in range(2):
                        split_lo(later(n, i + 1))
                        chunk = flat(h[:, at(t, 2, i)])
                        nc.vector.scalar_tensor_tensor(out=chunk, in0=product(later(n, i)), scalar=scale, in1=chunk,
                                                       op0=ALU.mult, op1=ALU.add).then_inc(bank_free[slot(later(n, i))], 1)

                def last_two(n, t):
                    for i in range(2):
                        split_lo(n + i + 1)
                        chunk = h[:, blocks - 2 + i]
                        nc.vector.scalar_tensor_tensor(out=chunk, in0=product(n + i), scalar=scale, in1=chunk,
                                                       op0=ALU.mult, op1=ALU.add).then_inc(bank_free[slot(n + i)], 1)

                if first + blocks == N_BLOCKS:
                    pairs(dve, first, blocks - 2, two)
                    last_two(N_BLOCKS - 2, None)
                else:
                    pairs(dve, first, blocks, two)

            def residual_of_norm(first, k, scale=1.0):
                for c in range(DC):
                    split_lo(first + c + 1)
                    nc.vector.scalar_tensor_tensor(out=h[:, c], in0=product(first + c), scalar=scale, in1=h[:, c],
                                                   op0=ALU.mult, op1=ALU.add).then_inc(bank_free[slot(first + c)], 1)
                    if c >= 1 and k != N_FINAL:
                        low(k, c - 1)
                if k != N_FINAL:
                    low(k, DC - 1)

            residual_of_norm(RUN_AT["sb_out"], N_MLP0)

            def hidden_lo(t, scale, plus, done, group):
                dve.wait_ge(sig("uh_done"), done)
                nc.vector.tensor_tensor(flat(u_lo[:, group % 2, at(t, scale, plus)]), u[:, plus],
                                        flat(u_hi[:, group % 2, at(t, scale, plus)]).bitcast(F32),
                                        ALU.subtract).then_inc(sig("ul_done"), 1)

            def mlp(first, chunks_before, norm, next_norm):
                def up(n, t, group, before):
                    for i in range(2):
                        split_lo(later(n, i + 1))
                        if t is None and i == 0 and group == 0:
                            inverse(norm)
                        scaled(later(n, i), u_act[:], 0.0, ALU.max)
                        hidden_lo(t, 2, i, count(t, 2, before + i + 1), group)
                groups(MLP_GROUPS, first, chunks_before, 1, up, 1.0, next_norm)

            def ffn(first, chunks_before, norm, next_norm):
                def up(n, t, group, before):
                    split_lo(later(n, 1))
                    if t is None and group == 0:
                        inverse(norm)
                    scaled(n, u_act[:])
                    split_lo(later(n, 2))
                    dve.wait_ge(sig("ul_done"), count(t, 1, before))
                    m = later(n, 1)
                    scaled(m, u[:, 0])
                    dve.wait_ge(bank_free[slot(m)], turn(m, 2))
                    dve.wait_ge(sig("silu_done"), count(t, 1, before + 1 - 2 * HIDDEN // P))
                    nc.vector.tensor_tensor(u[:, 0], u[:, 0], u_act[:], ALU.mult).then_inc(sig("u_done"), 1)
                    dve.wait_ge(sig("u_done"), count(t, 1, before + 1))
                    hidden_lo(t, 1, 0, count(t, 1, before + 1), group)
                groups(FFN_GROUPS, first, chunks_before, 2, up, 0.5, next_norm)

            def groups(sizes, first, chunks_before, per_chunk, up, scale, next_norm):
                n = first
                for g in range(len(sizes) + 1):
                    if g < len(sizes):
                        before = chunks_before + sum(sizes[:g])
                        pairs(dve, n, sizes[g] * per_chunk, lambda m, t: up(m, t, g, before), peel=(g == 0))
                        n += sizes[g] * per_chunk
                    if g == len(sizes) and next_norm is not None:
                        residual_of_norm(n, next_norm, scale)
                    elif g >= 1:
                        residual(n, DC, scale)
                        n += DC

            mlp(RUN_AT["mlp0"], 0, N_MLP0, N_MIX1)

            cos, sin = tab_ret[:, 0], tab_ret[:, 1]

            def step(name, made_at):
                dve.wait_ge(sig(name), made_at)

            def rotate(n, dst, t, i):
                scale = RET_QK ** -0.5 if dst is r_k else 1.0
                scaled(n, r_x[:, 0], scale)
                split_lo(later(n, 2))
                scaled(later(n, 1), r_x[:, 1], scale)
                for m in (n, later(n, 1)):
                    dve.wait_ge(bank_free[slot(m)], turn(m, 2))
                if t is not None or i:
                    step("rot_done", count(t, 2, i))
                first, second = r_x[:, 0], r_x[:, 1]
                for half, (a, b, op) in enumerate(((cos, sin, ALU.subtract), (sin, cos, ALU.add))):
                    if half:
                        step("rhalf_done", count(t, 2, i + 1))
                    nc.vector.tensor_tensor(r_t[:, 0], first, a, ALU.mult).then_inc(sig("rt_done"), 1)
                    nc.vector.tensor_tensor(r_t[:, 1], second, b, ALU.mult).then_inc(sig("rt_done"), 1)
                    step("rt_done", count(t, 8, 4 * i + 2 * half + 2))
                    last = nc.vector.tensor_tensor(dst[:, half], r_t[:, 0], r_t[:, 1], op)
                    last.then_inc(sig("rot_done") if half else sig("rhalf_done"), 1)

            def r_value(n, t, i, j):
                if j < 2:
                    step("rot_done", count(t, 2, 2 * i + 2))
                scaled(n, r_t[:, j % 2])

            def r_values(t, i, j):
                dve.wait_ge(sig("rvt_done"), count(t, 4, 4 * i + j + 1))
                nc.vector.tensor_copy(r_v[:, :, j * P:(j + 1) * P],
                                      ps[:, 4].rearrange("p (b f) -> p b f", b=TB)).then_inc(sig("rv_done"), 1)

            def r_head(n, t, i, dense=True):
                for kb in range(TB):
                    dve.wait_ge(sig("rs_done"), count(t, 1, i + 1))
                    nc.vector.tensor_tensor(r_p[:, S_AT[kb]:S_AT[kb] + seen_by(kb)], s_flat[:, S_AT[kb]:S_AT[kb] + seen_by(kb)],
                                            flat(tab_ret[:, at(t, 1, 2 + i), 0:seen_by(kb)]), ALU.mult).then_inc(sig("rp_done"), 1)
                if dense:
                    for j in range(2):
                        split_lo(later(n, 2 * j + 1))
                        rotate(later(n, 2 * j), (r_q, r_k)[j], t, 2 * (i + 1) + j)
                    for j in range(4):
                        split_lo(later(n, 4 + j + 1))
                        if j >= 2:
                            r_values(t, i + 1, j - 2)
                        r_value(later(n, 4 + j), t, i + 1, j)
                    r_values(t, i + 1, 2)
                gate = later(n, RET_QKV if dense else 0)
                for e in range(4):
                    dve.wait_ge(sig("rmu_done"), count(t, 1, i + 1))
                    nc.vector.tensor_tensor(r_o[:, e], r_o[:, e], ps[:, 5], ALU.subtract).then_inc(sig("cen_done"), 1)
                split_lo(later(gate, 1))
                scaled(gate, r_g[:, 0])
                if dense:
                    r_values(t, i + 1, 3)
                split_lo(later(gate, 2))
                scaled(later(gate, 1), r_g[:, 1])
                dve.wait_ge(sig("rstd_in"), count(t, 1, i + 1))
                nc.vector.reciprocal(r_sq[0], std[:]).then_inc(sig("rrstd_done"), 1)
                split_lo(later(gate, 3))
                scaled(later(gate, 2), r_g[:, 2])
                split_lo(later(gate, 4))
                scaled(later(gate, 3), r_g[:, 3])
                step("rrstd_done", count(t, 1, i + 1))
                for e in range(4):
                    nc.vector.tensor_tensor(r_o[:, e], r_o[:, e], r_sq[0], ALU.mult).then_inc(sig("rn_done"), 1)
                for e in range(4):
                    step("rn_done", count(t, 4, 4 * i + e + 1))
                    dve.wait_ge(sig("rgate_done"), count(t, 4, 4 * i + e + 1))
                    nc.vector.tensor_tensor(r_o[:, e], r_o[:, e], r_g[:, e], ALU.mult).then_inc(sig("ry_done"), 1)
                for e in range(4):
                    dve.wait_ge(sig("yh_done"), count(t, 4, 4 * i + e + 1))
                    nc.vector.tensor_tensor(flat(y_lo[:, at(t, 4, 4 * i + e)]), r_o[:, e],
                                            flat(y_hi[:, at(t, 4, 4 * i + e)]).bitcast(F32), ALU.subtract).then_inc(sig("yl_done"), 1)

            s_flat = ps[:, 0:3].rearrange("p a b -> p (a b)")
            dve.wait_ge(sig("tables_ret_in"), 16)
            first = RUN_AT["ret"]
            for j in range(2):
                split_lo(first + 2 * j + 1)
                if j == 0:
                    inverse(N_MIX1)
                rotate(first + 2 * j, (r_q, r_k)[j], None, j)
            for j in range(4):
                split_lo(first + 4 + j + 1)
                if j >= 2:
                    r_values(None, 0, j - 2)
                r_value(first + 4 + j, None, 0, j)
            r_values(None, 0, 2)
            r_values(None, 0, 3)
            pairs(dve, first + RET_QKV, 12 * (RET_HEADS - 1), lambda n, t: r_head(n, t, 0), step=12)
            r_head(RUN_AT["ret_out"] - RET_G, None, RET_HEADS - 1, dense=False)
            residual(RUN_AT["ret_out"], DC)
            residual_of_norm(RUN_AT["ret_out"] + DC, N_MLP1)
            mlp(RUN_AT["mlp1"], HIDDEN // P, N_MLP1, N_FINAL)
            inverse(N_FINAL)
            for c in range(DC):
                nc.vector.scalar_tensor_tensor(out=h[:, c], in0=h[:, c], scalar=col("g_final", c), in1=inv[:],
                                               op0=ALU.mult, op1=ALU.mult).then_inc(sig("final_done"), 1)
                if c >= 1:
                    low(N_FFN1, c - 1)
            low(N_FFN1, DC - 1)
            ffn(RUN_AT["ffn1"], 2 * HIDDEN // P, N_FFN1, N_MIX)

            def mix_two(n, t):
                for i in range(2):
                    split_lo(later(n, i + 1))
                    if t is None and i == 0:
                        inverse(N_MIX)
                    scaled(later(n, i), flat(pj[:, at(t, 2, MIX_GATES + i)]))

            pairs(dve, RUN_AT["mix"], MIX_BLOCKS - MIX_GATES - 1, mix_two, peel=True)
            split_lo(RUN_AT["mix_late"])
            scaled(RUN_AT["mix_late"] - 1, pj[:, MIX_BLOCKS - 1])
            dve.wait_ge(sig("vt_mix"), 5)
            nc.vector.tensor_scalar(iw[:], ps[:, 5].rearrange("p (b f) -> p b f", b=TB)[:, :, GATE_IW:GATE_IW + IDX_HEADS],
                                    IDX_DIM ** -0.5 * IDX_HEADS ** -0.5, None, ALU.mult).then_inc(sig("iw_done"), 1)
            def tap(c, i):
                return col("conv_w", c * CONV + i)

            steps = 0
            for c in range(4):
                mx, xc = pj[:, MIX_MX + c], m_xc[:, c]
                nc.vector.tensor_scalar(xc, mx, tap(c, CONV - 1), col("conv_b", c), ALU.mult, ALU.add).then_inc(sig("tap_done"), 1)
                for back in range(1, CONV):
                    steps += 1
                    step("tap_done", steps)
                    nc.vector.scalar_tensor_tensor(out=xc[:, back:T], in0=mx[:, 0:T - back], scalar=tap(c, CONV - 1 - back),
                                                   in1=xc[:, back:T], op0=ALU.mult, op1=ALU.add).then_inc(
                        sig("tap_done") if back < CONV - 1 else sig("conv_done"), 1)

            dve.wait_ge(sig("gate_done"), 2)
            nc.vector.scalar_tensor_tensor(out=g_sum[:], in0=g_lf[:], scalar=-1.0, in1=g_lf[:], op0=ALU.mult,
                                           op1=ALU.max).then_inc(sig("gabs_done"), 1)
            nc.vector.memset(g_max[:], 1.0).then_inc(sig("gone_done"), 1)
            dve.wait_ge(sig("gexp_done"), 2)
            nc.vector.scalar_tensor_tensor(out=g_lf[:], in0=g_lf[:], scalar=0.0, in1=g_sum[:], op0=ALU.min,
                                           op1=ALU.subtract).then_inc(sig("grow_done"), 1)
            step("grow_done", 1)
            step("gone_done", 1)
            nc.vector.tensor_tensor_scan(g_sum[:], g_max[:], g_lf[:], 0.0, ALU.mult, ALU.add).then_inc(sig("grow_done"), 1)
            step("grow_done", 2)
            nc.vector.tensor_tensor(g_a[:], g_li[:], g_sum[:], ALU.subtract).then_inc(sig("grow_done"), 1)
            step("grow_done", 3)
            nc.vector.tensor_tensor_scan(g_max[:], g_a[:], g_a[:], 0.0, ALU.max, ALU.max).then_inc(sig("grow_done"), 1)
            step("grow_done", 4)
            nc.vector.tensor_tensor(g_lf[:], g_max[:], g_sum[:], ALU.add).then_inc(sig("grow_done"), 1)

            for hd in range(ML_HEADS):
                late = RUN_AT["mix_late"] + LATE_PER_HEAD * hd
                split_lo(late + 1)
                dve.wait_ge(sig("mexp_done"), 8 * (hd + 1))
                dve.wait_ge(sig("mscore_done"), hd + 1)
                for kb in range(TB):
                    part = slice(S_AT[kb], S_AT[kb] + seen_by(kb))
                    nc.vector.tensor_tensor(m_w[:, part], s_flat[:, part], m_w[:, part], ALU.mult).then_inc(sig("mw_done"), 1)
                scaled(late, pj[:, LATE_PER_HEAD * hd])
                split_lo(late + 2)
                dve.wait_ge(sig("mnum_done"), hd + 1)
                nc.vector.scalar_tensor_tensor(out=rstd[:], in0=ps[:, 4], scalar=-1.0, in1=xn[:, 0], op0=ALU.mult,
                                               op1=ALU.max).then_inc(sig("mden_done"), 1)
                step("mden_done", 4 * hd + 1)
                nc.vector.tensor_tensor(rstd[:], ps[:, 4], rstd[:], ALU.max).then_inc(sig("mden_done"), 1)
                step("mden_done", 4 * hd + 2)
                nc.vector.reciprocal(rstd[:], rstd[:]).then_inc(sig("mden_done"), 1)
                step("mden_done", 4 * hd + 3)
                nc.vector.tensor_tensor(m_h[:], ps[:, 3], rstd[:], ALU.mult).then_inc(sig("mh_done"), 1)
                scaled(late + 1, pj[:, LATE_PER_HEAD * hd + 1])
                split_lo(late + 3)
                dve.wait_ge(sig("mstd_done"), hd + 1)
                step("mh_done", 3 * hd + 1)
                nc.vector.reciprocal(rstd[:], std[:]).then_inc(sig("mden_done"), 1)
                step("mden_done", 4 * hd + 4)
                nc.vector.scalar_tensor_tensor(out=m_h[:], in0=m_h[:], scalar=col("head_norm", hd), in1=rstd[:],
                                               op0=ALU.mult, op1=ALU.mult).then_inc(sig("mh_done"), 1)
                step("mh_done", 3 * hd + 2)
                dve.wait_ge(sig("mso_done"), hd + 1)
                nc.vector.tensor_tensor(m_h[:], m_h[:], m_so[:], ALU.mult).then_inc(sig("mh_done"), 1)
                dve.wait_ge(sig("yb_hi_done"), hd + 1)
                nc.vector.tensor_tensor(yb_lo[:, hd], m_h[:], yb_hi[:, hd].bitcast(F32), ALU.subtract).then_inc(sig("yb_lo_done"), 1)
                scaled(late + 2, pj[:, LATE_PER_HEAD * hd + 2])

            for j, (m, gain) in enumerate(HEAD_NORMED.items()):
                dve.wait_ge(sig("hstd_done"), j + 1)
                nc.vector.reciprocal(n_r[:, j % 2], n_std[:, j % 2]).then_inc(sig("hr_done"), 1)
                step("hr_done", j + 1)
                nc.vector.scalar_tensor_tensor(out=pj[:, m], in0=pj[:, m], scalar=col(gain), in1=n_r[:, j % 2],
                                               op0=ALU.mult, op1=ALU.mult).then_inc(sig("hn_done"), 1)

            step("hn_done", len(HEAD_NORMED))
            step("iw_done", 1)
            nc.vector.memset(neg[:, 0:P], 0.0).then_inc(sig("neg_done"), 1)
            step("neg_done", 1)
            nc.vector.memset(neg[0:CHUNK, CHUNK:P], -BIG).then_inc(sig("neg_done"), 1)
            for tb in range(1, TB):
                seen = (tb + 1) * P
                row = score[:, 0:seen]
                for hd in range(IDX_HEADS):
                    j = (tb - 1) * IDX_HEADS + hd
                    dve.wait_ge(sig("irelu_done"), j + 1)
                    weight = iw[:, tb, hd:hd + 1]
                    if hd == 0:
                        nc.vector.tensor_scalar(row, rr[:, j % 2, 0:seen], weight, None, ALU.mult).then_inc(sig("iacc_done"), 1)
                    else:
                        step("iacc_done", j)
                        nc.vector.scalar_tensor_tensor(out=row, in0=rr[:, j % 2, 0:seen], scalar=weight, in1=row,
                                                       op0=ALU.mult, op1=ALU.add).then_inc(sig("iacc_done"), 1)
                step("iacc_done", tb * IDX_HEADS)
                nc.vector.memset(score[0:CHUNK, seen - CHUNK:seen], OUT_OF_REACH).then_inc(sig("cut_done"), 1)
                step("cut_done", tb)

                def take(t):
                    base = (tb - 1) * (TOPK // 8)
                    nc.vector.max(best[:], row).then_inc(sig("best_done"), 1)
                    step("best_done", t + (base + 1))
                    nc.vector.match_replace(row, best[:], row, TAKEN).then_inc(sig("taken_done"), 1)
                    step("taken_done", t + (base + 1))

                for t in range(TOPK // 8):
                    i, part = divmod(t, TOPK // 8 // GATES_PER_SELECTION)
                    i += (tb - 1) * GATES_PER_SELECTION
                    if part == 0:
                        split_lo(RUN_AT["gates"] + i + 1)
                    take(t)
                    if part == TOPK // 8 // GATES_PER_SELECTION - 1:
                        scaled(RUN_AT["gates"] + i, pj[:, gate_chunk(i)])
                nc.vector.tensor_scalar(neg[:, NEG_AT[tb]:NEG_AT[tb] + seen], row, OUT_OF_REACH * 2, -BIG,
                                        ALU.is_gt, ALU.mult).then_inc(sig("neg_done"), 1)
                step("neg_done", tb + 2)

            def att_max(j):
                tb = j // 2 % TB
                seen = (tb + 1) * P
                dve.wait_ge(sig("as_done"), j + 1)
                if j >= 2:
                    dve.wait_ge(sig("aturn_done"), j - 1)
                nc.vector.tensor_tensor_reduce(out=s_m[:, j % 2, 0:seen], in0=ps[:, j % 2, 0:seen],
                                               in1=neg[:, NEG_AT[tb]:NEG_AT[tb] + seen], scale=1.0, scalar=TAKEN,
                                               op0=ALU.add, op1=ALU.max, accum_out=stat[:, 0, j:j + 1]).then_inc(sig("arow_done"), 1)
                step("arow_done", j + 1)
                nc.vector.tensor_scalar(stat[:, 1, j:j + 1], stat[:, 0, j:j + 1], -(ATT_DIM ** -0.5), None,
                                        ALU.mult).then_inc(sig("amax_done"), 1)

            def att_norm(j):
                seen = (j // 2 % TB + 1) * P
                dve.wait_ge(sig("aexp_done"), j + 1)
                nc.vector.reciprocal(stat[:, 3, j:j + 1], stat[:, 2, j:j + 1]).then_inc(sig("ainv_done"), 1)
                step("ainv_done", j + 1)
                nc.vector.tensor_scalar(s_m[:, j % 2, 0:seen], s_m[:, j % 2, 0:seen], stat[:, 3, j:j + 1], None,
                                        ALU.mult).then_inc(sig("anorm_done"), 1)

            n_att = ATT_HEADS * TB
            for j in range(n_att + 1):
                if j in GATE_STEPS:
                    split_lo(RUN_AT["proj"] - len(GATE_STEPS) + GATE_STEPS.index(j) + 1)
                if j < n_att:
                    att_max(j)
                if j >= 1:
                    att_norm(j - 1)
                if j - 1 in GATE_STEPS:
                    i = 2 * DC - len(GATE_STEPS) + GATE_STEPS.index(j - 1)
                    scaled(RUN_AT["gates"] + i, pj[:, gate_chunk(i)])
                if j >= 9 and (j - 2) % 8 == 7 or j == n_att:
                    c = (j - 2) // 8 if j < n_att else 3
                    dve.wait_ge(sig("ya_hi_done"), c + 1)
                    nc.vector.tensor_tensor(ya_lo[:, c], ps[:, 4 + c % 2], ya_hi[:, c].bitcast(F32),
                                            ALU.subtract).then_inc(sig("ya_lo_done"), 1)

            for m in range(DC):
                n = RUN_AT["proj"] + m
                split_lo(n + 1)
                dve.wait_ge(sig("mgate_done"), 2 * m + 2)
                if m:
                    step("mg_lo_done", m)
                nc.vector.tensor_tensor(std[:], product(n), xn[:, 0], ALU.mult).then_inc(bank_free[slot(n)], 1)
                nc.vector.tensor_tensor(u_sum[:], ps[:, 5], xn[:, 1], ALU.mult).then_inc(sig("mgb_done"), 1)
                dve.wait_ge(bank_free[slot(n)], turn(n, 2))
                step("mgb_done", m + 1)
                nc.vector.tensor_tensor(u_sum[:], std[:], u_sum[:], ALU.add).then_inc(sig("mg_done"), 1)
                dve.wait_ge(sig("mg_hi_done"), m + 1)
                nc.vector.tensor_tensor(mg_lo[:, m], u_sum[:], mg_hi[:, m].bitcast(F32), ALU.subtract).then_inc(sig("mg_lo_done"), 1)

            residual_of_norm(RUN_AT["w_out"], N_FFN2)
            ffn(RUN_AT["ffn2"], 2 * HIDDEN // P + D_FF // P, N_FFN2, None)

        @block.gpsimd
        def _(pool):
            for t, value in ((mean_d, 1 / D), (mean_v, 1 / RET_V), (one, 1.0), (neg_one, -1.0), (eps[:], EPS)):
                nc.gpsimd.memset(t, value).then_inc(sig("consts"), 1)
            for k in range(len(NORMS)):
                for c in range(DC):
                    pool.wait_ge(sig("sq_done"), k * DC + c + 1)
                    if c == 0:
                        nc.gpsimd.tensor_copy(sq_sum[:], xn[:, 0]).then_inc(sig("sum_done"), 1)
                    else:
                        pool.wait_ge(sig("sum_done"), k * DC + c)
                        nc.gpsimd.tensor_tensor(sq_sum[:], sq_sum[:], xn[:, c % 2], ALU.add).then_inc(sig("sum_done"), 1)

        @block.tensor
        def _(pe):
            pe.sem_inc(mm_done, 2)

            def dense(n, hi, lo, kc=KC):
                pe.wait_ge(lo_done, number(n, 3))
                pe.wait_ge(bank_free[slot(n)], turn(n, 1))
                s = slot(n)
                for k in range(kc):
                    for i, (w, x) in enumerate(((w_hi, hi), (w_hi, lo), (w_lo, hi))):
                        last = nc.tensor.matmul(ps[:, GEMM_BANK + s], w[:, s, k], x(k), start=(k == 0 and i == 0),
                                                stop=(k == kc - 1 and i == 2))
                last.then_inc(mm_done, 1)

            def count(t, scale, plus):
                return plus if t is None else t * scale + plus

            def of_x(n):
                dense(n, lambda k: x_hi[:, k], lambda k: x_lo[:, k])

            split_norms = [k for k in range(len(NORMS)) if k != N_FINAL]

            def mean_square(k):
                pe.wait_ge(sig("sum_done"), (k + 1) * DC)
                nc.tensor.matmul(ps[:, 5], mean_d, sq_sum[:], start=True, stop=True).then_inc(sig("ms_done"), 1)

            def of_new_x(n, k):
                pe.wait_ge(lo_done, number(n, 3))
                pe.wait_ge(bank_free[slot(n)], turn(n, 1))
                s = slot(n)
                for c in range(DC):
                    if c == DC - 1:
                        mean_square(k)
                    pe.wait_ge(sig("xl_done"), split_norms.index(k) * DC + c + 1)
                    for i, (w, x) in enumerate(((w_hi, x_hi), (w_hi, x_lo), (w_lo, x_hi))):
                        last = nc.tensor.matmul(ps[:, GEMM_BANK + s], w[:, s, c], x[:, c], start=(c == 0 and i == 0),
                                                stop=(c == DC - 1 and i == 2))
                last.then_inc(mm_done, 1)

            def turn_block(dst, src):
                return nc.tensor.transpose(dst, src, ident)

            pe.wait_ge(sig("x_in"), 16)
            pe.wait_ge(sig("tables_in"), 32)
            for c in range(DC):
                if c >= 4:
                    pe.wait_ge(sig("h_in"), c - 3)
                for b in range(TB):
                    last = turn_block(ps[:, c % 4, b * P:(b + 1) * P], x_tok[:, b, c * P:(c + 1) * P])
                last.then_inc(sig("x_turned"), 1)
            pe.wait_ge(sig("consts"), 5)

            z_flat = ps[:, 0:Z_BANKS].rearrange("p a b -> p (a b)")
            sp_flat = z_sp[:].rearrange("p a b -> p (a b)")
            a_flat = z_ex[:].rearrange("p a b -> p (a b)")

            def moved(n):
                pe.wait_ge(bank_free[slot(n)], turn(n, 2))

            def sb_turn(n):
                moved(n)
                for b in range(TB):
                    last = turn_block(ps[:, 4, b * P:(b + 1) * P], sb_v[:, b * P:(b + 1) * P])
                last.then_inc(sig("sbvt_done"), 1)

            def sb_scores(n, p):
                moved(later(n, 1))
                pe.wait_ge(sig("sbv_done"), p)
                for hd in range(2):
                    rows = slice(hd * SB_DIM, (hd + 1) * SB_DIM)
                    for kb in (2, 0, 1, 3) if hd == 0 else (0, 1, 3, 2):
                        c = Z_AT[hd, kb]
                        if hd == 1 and kb == 2:
                            pe.wait_ge(sig("z_shared_done"), p)
                        nc.tensor.matmul(z_flat[:, c:c + seen_by(kb)], sb_k[rows, kb * P:(kb + 1) * P],
                                         sb_q[rows, kb * P:T], start=(c % T == 0), stop=False, skip_group_check=True)
                        last = nc.tensor.matmul(z_flat[:, c:c + P], ident, strict, start=False, stop=False,
                                                skip_group_check=True)
                        if hd == 0 and kb == 2:
                            last.then_inc(sig("z_shared_done"), 1)
                last.then_inc(sig("z_done"), 1)

            def sb_sums(p):
                pe.wait_ge(sig("sp_done"), p)
                for hd in range(2):
                    for kb in range(TB):
                        for jb in range(kb, TB):
                            c = Z_AT[hd, kb] + (jb - kb) * P
                            src = Z_AT[hd, jb]
                            last = nc.tensor.matmul(z_flat[:, c:c + seen_by(jb)], neg_tri if jb == kb else neg_one,
                                                    sp_flat[:, src:src + seen_by(jb)], start=False, stop=(jb == TB - 1),
                                                    skip_group_check=True)
                last.then_inc(sig("cum_done"), 1)

            def sb_out(p):
                pe.wait_ge(sig("a_done"), p)
                for hd in range(2):
                    rows = slice(hd * SB_DIM, (hd + 1) * SB_DIM)
                    for kb in range(TB):
                        c = Z_AT[hd, kb]
                        last = nc.tensor.matmul(ps[rows, 5, kb * P:T], sb_vt[:, kb, rows], a_flat[:, c:c + seen_by(kb)],
                                                start=(kb == 0), stop=(kb == TB - 1), skip_group_check=True)
                last.then_inc(sig("av_done"), 1)

            of_new_x(0, N_MIX0)
            of_x(1)
            of_x(2)
            sb_turn(2)

            def sb_pair(n, t, pc, step, dense_=True):
                sb_scores(later(n, -3), count(t, step, pc + 1))
                if dense_:
                    of_x(n)
                    of_x(later(n, 1))
                sb_sums(count(t, step * Z_BANKS, (pc + 1) * Z_BANKS))
                if dense_:
                    of_x(later(n, 2))
                sb_out(count(t, step * Z_BANKS, (pc + 1) * Z_BANKS))
                if dense_:
                    sb_turn(later(n, 2))

            def sb_two(n, t):
                sb_pair(n, t, 0, 2)
                sb_pair(later(n, 3), t, 1, 2)

            pairs(pe, 3, 6 * 3, sb_two, step=6)
            sb_pair(3 * 7, None, 6, 0)
            sb_pair(3 * 8, None, 7, 0, dense_=False)

            def run(first, blocks, hi, lo, kc=KC):
                def two(n, _):
                    dense(n, hi, lo, kc)
                    dense(later(n, 1), hi, lo, kc)
                pairs(pe, first, blocks, two)

            pe.wait_ge(sig("ol_done"), DC)
            run(RUN_AT["sb_out"], DC, lambda k: o_hi[:, k], lambda k: o_lo[:, k])

            def groups(sizes, first, chunks_before, per_chunk, norm):
                n = first
                for g in range(len(sizes) + 1):
                    if g < len(sizes):
                        new = 2 if g == 0 else 0
                        if g == 0:
                            of_new_x(n, norm)
                            of_x(n + 1)
                        run(n + new, sizes[g] * per_chunk - new, lambda k: x_hi[:, k], lambda k: x_lo[:, k])
                        n += sizes[g] * per_chunk
                    if g >= 1:
                        b = (g - 1) % 2
                        pe.wait_ge(sig("ul_done"), chunks_before + sum(sizes[:g]))
                        run(n, DC, lambda k: u_hi[:, b, k], lambda k: u_lo[:, b, k], sizes[g - 1])
                        n += DC

            groups(MLP_GROUPS, RUN_AT["mlp0"], 0, 1, N_MLP0)

            s_flat = ps[:, 0:3].rearrange("p a b -> p (a b)")

            def r_turn(n, j):
                moved(n)
                for b in range(TB):
                    last = turn_block(ps[:, 4, b * P:(b + 1) * P], r_t[:, j % 2, b * P:(b + 1) * P])
                last.then_inc(sig("rvt_done"), 1)

            def r_head(n, t, i, dense_=True):
                pe.wait_ge(sig("rot_done"), count(t, 2, 2 * i + 2))
                for kb in (0, 1, 3, 2):
                    c = S_AT[kb]
                    for k in range(2):
                        last = nc.tensor.matmul(s_flat[:, c:c + seen_by(kb)], r_k[:, k, kb * P:(kb + 1) * P], r_q[:, k, kb * P:T],
                                                start=(c % T == 0 and k == 0), stop=(k == 1), skip_group_check=True)
                last.then_inc(sig("rs_done"), 1)
                if dense_:
                    for j in range(4):
                        of_x(later(n, j))
                pe.wait_ge(sig("rp_done"), count(t, 4, 4 * i + 4))
                pe.wait_ge(sig("rv_done"), count(t, 4, 4 * i + 4))
                for e in range(4):
                    for kb in range(TB):
                        c = S_AT[kb]
                        last = nc.tensor.matmul(ps[:, e, kb * P:T], r_v[:, kb, e * P:(e + 1) * P], r_p[:, c:c + seen_by(kb)],
                                                start=(kb == 0), stop=(kb == TB - 1))
                    last.then_inc(sig("rav_done"), 1)
                if dense_:
                    for j in range(4):
                        of_x(later(n, 4 + j))
                        if j >= 1:
                            if j >= 2:
                                pe.wait_ge(sig("rv_done"), count(t, 4, 4 * (i + 1) + j - 1))
                            r_turn(later(n, 4 + j - 1), j - 1)
                pe.wait_ge(sig("ro_done"), count(t, 4, 4 * i + 4))
                for e in range(4):
                    last = nc.tensor.matmul(ps[:, 5], mean_v, r_o[:, e], start=(e == 0), stop=(e == 3))
                last.then_inc(sig("rmu_done"), 1)
                gate = later(n, RET_QKV if dense_ else 0)
                of_x(gate)
                if dense_:
                    pe.wait_ge(sig("rv_done"), count(t, 4, 4 * (i + 1) + 3))
                    r_turn(later(n, 7), 3)
                of_x(later(gate, 1))
                pe.wait_ge(sig("cen_done"), count(t, 4, 4 * i + 4))
                for e in range(4):
                    pe.wait_ge(sig("rsq_done"), count(t, 4, 4 * i + e + 1))
                    nc.tensor.matmul(ps[:, 5], mean_v, r_sq[e], start=(e == 0), stop=(e == 3)).then_inc(sig("rvar_done"), 1)
                of_x(later(gate, 2))
                of_x(later(gate, 3))

            first = RUN_AT["ret"]
            for j in range(8):
                if j == 0:
                    of_new_x(first, N_MIX1)
                else:
                    of_x(first + j)
                if j >= 5:
                    if j >= 6:
                        pe.wait_ge(sig("rv_done"), j - 5)
                    r_turn(first + j - 1, j - 5)
            pe.wait_ge(sig("rv_done"), 3)
            r_turn(first + 7, 3)
            pairs(pe, first + RET_QKV, 12 * (RET_HEADS - 1), lambda n, t: r_head(n, t, 0), step=12)
            r_head(RUN_AT["ret_out"] - RET_G, None, RET_HEADS - 1, dense_=False)
            pe.wait_ge(sig("yl_done"), 2 * DC)
            for half in range(2):
                run(RUN_AT["ret_out"] + half * DC, DC, lambda k: y_hi[:, half * DC + k], lambda k: y_lo[:, half * DC + k])
            groups(MLP_GROUPS, RUN_AT["mlp1"], HIDDEN // P, 1, N_MLP1)
            mean_square(N_FINAL)
            groups(FFN_GROUPS, RUN_AT["ffn1"], 2 * HIDDEN // P, 2, N_FFN1)

            of_new_x(RUN_AT["mix"], N_MIX)
            of_x(RUN_AT["mix"] + 1)
            run(RUN_AT["mix"] + 2, MIX_BLOCKS - MIX_GATES - 3, lambda k: x_hi[:, k], lambda k: x_lo[:, k])
            of_x(RUN_AT["mix_late"] - 1)

            def turn_chunk(bank, m):
                moved(mix_block(m))
                for b in range(TB):
                    last = turn_block(ps[:, bank, b * P:(b + 1) * P], pj[:, m, b * P:(b + 1) * P])
                last.then_inc(sig("vt_mix"), 1)

            for i, m in enumerate((MIX_MV, MIX_MV + 1, MIX_MV + 2, MIX_MV + 3, MIX_GATES)):
                turn_chunk(1 + i, m)
            moved(RUN_AT["mix_late"] - 2)
            moved(RUN_AT["mix_late"] - 1)
            pe.wait_ge(sig("vt_moved"), 4)
            pe.wait_ge(sig("iw_done"), 1)
            pe.wait_ge(sig("grow_done"), 5)
            pe.wait_ge(sig("tables_mix_in"), 16)
            for b in range(TB):
                last = nc.tensor.transpose(ps[:, 0, b * ML_HEADS:(b + 1) * ML_HEADS], g_a[:, b * P:(b + 1) * P],
                                           ident[0:ML_HEADS, 0:ML_HEADS])
            last.then_inc(sig("ma_in"), 1)
            pe.wait_ge(sig("ma_done"), 1)
            for hd in range(ML_HEADS):
                if hd:
                    pe.wait_ge(sig("mh_done"), 3 * hd)
                pe.wait_ge(sig("xc_done"), 4)
                for i in range(2):
                    c = PARAMS["w_mqk"][0] + (2 * hd + i) * ML_QK
                    last = nc.tensor.matmul(ps[0:ML_QK, 1 + i], prm[:, c:c + ML_QK], m_xc[:, hd], start=True, stop=True)
                last.then_inc(sig("mqk_done"), 1)
                pick = tab_mix[0:ML_HEADS, hd]
                nc.tensor.matmul(ps[:, 3], pick, g_max[:], start=True, stop=True)
                nc.tensor.matmul(ps[:, 4], pick, g_max[:], start=True, stop=True, skip_group_check=True)
                for kb in range(TB):
                    nc.tensor.matmul(ps[:, 4, kb * P:(kb + 1) * P], ident, later_keys, start=False, stop=True,
                                     skip_group_check=True)
                nc.tensor.matmul(ps[:, 5], pick, g_lf[:], start=True, stop=True).then_inc(sig("mmax_done"), 1)
                pe.wait_ge(sig("mq_moved"), 2 * hd + 2)
                for kb in (0, 1, 3, 2):
                    c = S_AT[kb]
                    last = nc.tensor.matmul(s_flat[:, c:c + seen_by(kb)], m_k[:, kb * P:(kb + 1) * P], m_q[:, kb * P:T],
                                            start=(c % T == 0), stop=True, skip_group_check=True)
                last.then_inc(sig("mscore_done"), 1)
                late = RUN_AT["mix_late"] + LATE_PER_HEAD * hd
                of_x(late)
                pe.wait_ge(sig("mw_done"), 4 * hd + 4)
                for bank, lhs in ((3, lambda kb: m_v[:, kb, hd * P:(hd + 1) * P]), (4, lambda kb: one)):
                    for kb in range(TB):
                        c = S_AT[kb]
                        last = nc.tensor.matmul(ps[:, bank, kb * P:T], lhs(kb), m_w[:, c:c + seen_by(kb)],
                                                start=(kb == 0), stop=(kb == TB - 1))
                last.then_inc(sig("mnum_done"), 1)
                of_x(late + 1)
                pe.wait_ge(sig("msq_done"), hd + 1)
                nc.tensor.matmul(ps[:, 0], mean_h, xn[:, 1], start=True, stop=True).then_inc(sig("mvar_done"), 1)
                of_x(late + 2)

            moved(RUN_AT["gates"] - 2)
            moved(RUN_AT["gates"] - 1)
            pe.wait_ge(sig("yb_lo_done"), ML_HEADS)
            turn_chunk(0, MIX_V)
            pe.wait_ge(sig("vt_moved"), 5)
            for j in range(len(HEAD_NORMED)):
                pe.wait_ge(sig("hsq_done"), j + 1)
                if j >= 2:
                    pe.wait_ge(sig("hstd_done"), j - 1)
                nc.tensor.matmul(ps[:, j % 2], head_mean, n_sq[:, j % 2], start=True, stop=True).then_inc(sig("hms_done"), 1)

            pe.wait_ge(sig("hn_done"), len(HEAD_NORMED))
            for j in range(3 * IDX_HEADS):
                tb, hd = 1 + j // IDX_HEADS, j % IDX_HEADS
                rows = slice(hd % 2 * IDX_DIM, (hd % 2 + 1) * IDX_DIM)
                if j >= 2:
                    pe.wait_ge(sig("irelu_done"), j - 1)
                nc.tensor.matmul(ps[:, j % 2, 0:(tb + 1) * P], pj[rows, MIX_IQ + hd // 2, tb * P:(tb + 1) * P],
                                 pj[rows, MIX_IK, 0:(tb + 1) * P], start=True, stop=True).then_inc(sig("ilog_done"), 1)
                if j % IDX_HEADS == IDX_HEADS - 1:
                    for i in range(GATES_PER_SELECTION):
                        of_x(RUN_AT["gates"] + j // IDX_HEADS * GATES_PER_SELECTION + i)
            pe.wait_ge(sig("irelu_done"), 3 * IDX_HEADS)

            def att_scores(j):
                c, tb, hd = j // 8, j // 2 % TB, j % 2
                rows = slice(hd * ATT_DIM, (hd + 1) * ATT_DIM)
                if j >= 2:
                    pe.wait_ge(sig("amax_done"), j - 1)
                kv = (2 * c + hd) // (ATT_HEADS // ATT_KV)
                nc.tensor.matmul(ps[:, j % 2, 0:(tb + 1) * P], pj[rows, MIX_Q + c, tb * P:(tb + 1) * P],
                                 pj[rows, MIX_K + kv, 0:(tb + 1) * P], start=True, stop=True).then_inc(sig("as_done"), 1)

            def att_turn(j):
                tb = j // 2 % TB
                pe.wait_ge(sig("anorm_done"), j + 1)
                if j >= 2:
                    pe.wait_ge(sig("pt_done"), j - 1)
                for kb in range(tb + 1):
                    last = turn_block(ps[:, 2 + j % 2, kb * P:(kb + 1) * P], s_m[:, j % 2, kb * P:(kb + 1) * P])
                last.then_inc(sig("aturn_done"), 1)

            def att_out(j):
                c, tb, hd = j // 8, j // 2 % TB, j % 2
                kv = (2 * c + hd) // (ATT_HEADS // ATT_KV)
                pe.wait_ge(sig("pt_done"), j + 1)
                if c >= 2 and j % 8 == 0:
                    pe.wait_ge(sig("ya_lo_done"), c - 1)
                for kb in range(tb + 1):
                    last = nc.tensor.matmul(ps[hd * ATT_DIM:(hd + 1) * ATT_DIM, 4 + c % 2, tb * P:(tb + 1) * P],
                                            a_v[:, kb, kv * ATT_DIM:(kv + 1) * ATT_DIM], rr[:, j % 2, kb * P:(kb + 1) * P],
                                            start=(kb == 0), stop=(kb == tb), skip_group_check=True)
                last.then_inc(sig("apv_done"), 1)

            n_att = ATT_HEADS * TB
            for j in range(n_att + 2):
                if j < n_att:
                    att_scores(j)
                if 1 <= j <= n_att:
                    att_turn(j - 1)
                if j >= 2:
                    att_out(j - 2)
                if j in GATE_STEPS:
                    of_x(RUN_AT["proj"] - len(GATE_STEPS) + GATE_STEPS.index(j))

            pe.wait_ge(sig("ya_lo_done"), 4)
            for m in range(DC):
                n = RUN_AT["proj"] + m
                pe.wait_ge(lo_done, number(n, 3))
                pe.wait_ge(bank_free[slot(n)], turn(n, 1))
                if m:
                    pe.wait_ge(sig("mgb_done"), m)
                for bank, k0, hi, lo in ((GEMM_BANK + slot(n), 0, ya_hi, ya_lo), (5, 4, yb_hi, yb_lo)):
                    for k in range(4):
                        for i, (w, x) in enumerate(((w_hi, hi), (w_hi, lo), (w_lo, hi))):
                            last = nc.tensor.matmul(ps[:, bank], w[:, slot(n), k0 + k], x[:, k],
                                                    start=(k == 0 and i == 0), stop=(k == 3 and i == 2))
                last.then_inc(mm_done, 1)
            pe.wait_ge(sig("mg_lo_done"), DC)
            run(RUN_AT["w_out"], DC, lambda k: mg_hi[:, k], lambda k: mg_lo[:, k])
            groups(FFN_GROUPS, RUN_AT["ffn2"], 2 * HIDDEN // P + D_FF // P, 2, N_FFN2)

            moved(N_BLOCKS - 2)
            moved(N_BLOCKS - 1)
            for i in range(2 * TB):
                if i >= 4:
                    pe.wait_ge(sig("out_ready"), i - 3)
                for q in range(4):
                    last = turn_block(ps[:, i % 4, q * P:(q + 1) * P], h[:, i % 2 * 4 + q, i // 2 * P:(i // 2 + 1) * P])
                last.then_inc(sig("out_turned"), 1)



def weight_block(w, rows, cols):
    out = np.zeros((KC, P, P), np.float32)
    part = w[rows, cols]
    out[:part.shape[0] // P] = part.reshape(-1, P, part.shape[1])
    return out


def weight_stream(a):
    blocks = []

    def take(w, c, row=0, chunks=KC):
        blocks.append(weight_block(w, slice(row * P, (row + chunks) * P), slice(c * P, (c + 1) * P)))

    sb_in = a["w_sb_in"][0]
    for p in range(DC):
        for which in range(3):
            take(sb_in, which * DC + p)
    for m in range(DC):
        take(a["w_sb_out"][0], m)

    def mlp(ups, down, sizes):
        for g in range(len(sizes) + 1):
            if g < len(sizes):
                for m in range(sum(sizes[:g]), sum(sizes[:g + 1])):
                    for up in ups:
                        take(up, m)
            if g >= 1:
                for m in range(DC):
                    take(down, m, sum(sizes[:g - 1]), sizes[g - 1])

    mlp([a["w_mlp_up"][0]], a["w_mlp_down"][0], MLP_GROUPS)
    ret = a["w_ret_in"][0]

    def qkv(hd):
        for c in (2 * hd, 2 * hd + 1, DC + 2 * hd, DC + 2 * hd + 1):
            take(ret, c)
        for e in range(4):
            take(ret, 2 * DC + 4 * hd + e)

    qkv(0)
    for hd in range(RET_HEADS):
        if hd + 1 < RET_HEADS:
            qkv(hd + 1)
        for e in range(4):
            take(ret, 4 * DC + 4 * hd + e)
    for half in range(2):
        for m in range(DC):
            take(a["w_ret_out"][0], m, half * DC)
    mlp([a["w_mlp_up"][1]], a["w_mlp_down"][1], MLP_GROUPS)
    mlp([a["ffn1_w_gate_2"][0], a["ffn1_w_up_2"][0]], a["ffn1_w_down_2"][0], FFN_GROUPS)

    w_in = a["w_in_2"][0]
    widths = (512, 128, 128, 512, 64, 8, 512, 512, 4, 4, 512, 1024, 1024)
    aq, ak, av, iq, ik, iw, mx, mv, mi, mf, mo, ga, gb = np.cumsum((0,) + widths[:-1])

    def pick(cols):
        blocks.append(w_in[:, np.asarray(cols)].reshape(KC, P, P))

    def span(start, n=P):
        return list(range(start, start + n))

    pick(span(iw, 32) + span(mi, 32) + span(mf, 64))
    for start in (mx, mv, mo):
        for c in range(4):
            pick(span(start + c * P))
    for g in range(ATT_KV):
        pick(span(ak + g * ATT_DIM, ATT_DIM) * 2)
    for c in range(4):
        pick(span(aq + c * P))
    pick(span(av))
    pick(span(ik, IDX_DIM) * 2)
    for c in range(4):
        pick(span(iq + c * P))
    both = np.concatenate([a["w_proj_a_2"][0], a["w_proj_b_2"][0]], axis=0)
    for m in range(DC):
        pick(span(ga + m * P))
        pick(span(gb + m * P))
    for m in range(DC):
        take(both, m)
    for m in range(DC):
        take(a["w_out_2"][0], m)
    mlp([a["ffn2_w_gate_2"][0], a["ffn2_w_up_2"][0]], a["ffn2_w_down_2"][0], FFN_GROUPS)
    assert len(blocks) == N_BLOCKS
    return np.ascontiguousarray(np.stack(blocks).transpose(0, 2, 1, 3).reshape(N_BLOCKS, P, KC * P))


def small_params(a):
    out = np.zeros((P, n_param), np.float32)

    def put(name, value):
        c, n = PARAMS[name]
        out[:value.shape[0], c:c + n] = value

    for name, gain in (("g_mix0", a["g_mix"][0]), ("g_mix1", a["g_mix"][1]), ("g_mlp0", a["g_mlp"][0]),
                       ("g_mlp1", a["g_mlp"][1]), ("g_final", a["g_final"]), ("ffn1_norm", a["ffn1_norm_2"][0]),
                       ("mix_norm", a["mix_norm_2"][0]), ("ffn2_norm", a["ffn2_norm_2"][0])):
        put(name, gain.reshape(DC, P).T)
    for name in ("q_norm", "k_norm", "idx_k_norm"):
        put(name, np.concatenate([a[name + "_2"][0]] * 2)[:, None])
    put("conv_w", a["conv_w_2"][0].reshape(CONV, 4, P).transpose(2, 1, 0).reshape(P, 4 * CONV))
    put("conv_b", a["conv_b_2"][0].reshape(4, P).T)
    put("b_i", a["b_i_2"][0][:, None])
    put("b_f", a["b_f_2"][0][:, None])
    put("head_norm", a["m_head_norm_2"][0].reshape(ML_HEADS, P).T)
    put("w_mqk", np.stack([a["w_mq_2"][0], a["w_mk_2"][0]], axis=1).transpose(2, 0, 1, 3).reshape(P, -1))
    return out


def shape_tables():
    i = np.arange(P)
    common = np.zeros((P, 4, P), np.float32)
    common[:, 0] = np.eye(P)
    common[:, 1] = -(i[:, None] >= i[None, :]).astype(np.float32)
    common[:, 2] = -BIG * (i[:, None] >= i[None, :])
    common[:, 3] = (i[:, None] // ATT_DIM == i[None, :] // ATT_DIM) / ATT_DIM
    ret = np.zeros((P, 2 + RET_HEADS, T), np.float32)
    half = RET_QK // 2
    inv_freq = (1.0 / (10000.0 ** np.linspace(0.0, 1.0, half, dtype=np.float32))).astype(np.float32)
    angle = inv_freq[:, None] * np.arange(T, dtype=np.float32)[None, :]
    ret[:, 0], ret[:, 1] = np.cos(angle), np.sin(angle)
    rel = (np.arange(T)[None, :] - i[:, None]).astype(np.float64)
    for hd in range(RET_HEADS):
        log_gamma = float(np.log1p(-np.exp2(np.float32(-5.0 - hd))))
        ret[:, 2 + hd] = np.where(rel >= 0, np.exp(log_gamma * np.maximum(rel, 0)), 0)
    mix = np.zeros((P, 6, P), np.float32)
    for hd in range(ML_HEADS):
        mix[hd, hd] = 1.0
    mix[:, 4] = BIG * (i[:, None] > i[None, :])
    mix[:, 5] = 1.0 / ML_V
    return common, ret, mix


def kernel(**inputs):
    import concourse.bacc as bacc
    from concourse.bass_utils import run_bass_kernel_spmd

    a = {name: np.asarray(value) for name, value in inputs.items()}
    common, ret, mix = shape_tables()
    arrays = {"in_stream": weight_stream(a), "in_params": small_params(a), "in_tables": common,
              "in_tables_ret": ret, "in_tables_mix": mix, "in_x": np.ascontiguousarray(a["x"][0])}
    nc = bacc.Bacc("TRN2", target_bir_lowering=False, num_devices=1)
    aps = [nc.dram_tensor(name, value.shape, F32, kind="ExternalInput").ap() for name, value in arrays.items()]
    out = nc.dram_tensor("out_x", (T, D), F32, kind="ExternalOutput").ap()
    build(nc, *aps, out)
    result = run_bass_kernel_spmd(nc, [arrays], core_ids=[0])
    return result.results[0]["out_x"].reshape(1, T, D)
```
